# Optimizing a Trainium2 kernel written in Bass

```python
import math
import jax, jax.numpy as jnp
from jax import lax
import numpy as np

D_MODEL = 1024
BATCH = 1
SEQ = 256
DEPTH = 2

MEM_LEN = 256
EPS = 1e-6
SB_HEADS = 8
SB_HEAD_DIM = 64
SB_WIDTH = SB_HEADS * SB_HEAD_DIM
SB_BLOCK = 128
GLA_HEADS = 4
GLA_DK = 64
GLA_DV = 128
GLA_KW = GLA_HEADS * GLA_DK
GLA_VW = GLA_HEADS * GLA_DV
GLA_GATE_RANK = 16
GLA_GATE_TAU = 16.0
GLA_CHUNK = 64
CA_HEADS = 4
CA_HEAD_DIM = 128
CA_WIDTH = CA_HEADS * CA_HEAD_DIM
N_BRANCH = 3
IN_SPLITS = (SB_WIDTH, SB_WIDTH, SB_WIDTH, GLA_KW, GLA_KW, GLA_VW, GLA_GATE_RANK, GLA_VW, CA_WIDTH, N_BRANCH * D_MODEL)
IN_WIDTH = 3 * SB_WIDTH + 2 * GLA_KW + 2 * GLA_VW + GLA_GATE_RANK + CA_WIDTH + N_BRANCH * D_MODEL
D_FF = 2816
N_EXPERTS = 8
TOP_K = 2
D_FF_EXPERT = 3584
N_DENSE = (DEPTH + 1) // 2
N_MOE = DEPTH // 2

kernel_name = 'hybrid_sb_gla_memxattn_moe_trunk'

def rms_norm(x, g):
    xf = x.astype(jnp.float32)
    y = xf * lax.rsqrt(jnp.mean(xf * xf, axis=-1, keepdims=True) + EPS)
    return (y * g.astype(jnp.float32)).astype(x.dtype)

def split_heads(t, n):
    b, s, w = t.shape
    return t.reshape(b, s, n, w // n).transpose(0, 2, 1, 3)

def merge_heads(t):
    b, h, s, d = t.shape
    return t.transpose(0, 2, 1, 3).reshape(b, s, h * d)

def stick_breaking_attention(q, k, v):
    s_len, d = q.shape[2], q.shape[3]
    scale = d ** -0.5
    outs = []
    for i in range(s_len // SB_BLOCK):
        q0 = i * SB_BLOCK
        q1 = q0 + SB_BLOCK
        qb = q[:, :, q0:q1].astype(jnp.float32)
        kb = k[:, :, :q1].astype(jnp.float32)
        z = jnp.einsum('bhtd,bhsd->bhts', qb, kb) * scale
        causal = jnp.arange(q1)[None, :] < jnp.arange(q0, q1)[:, None]
        log_beta = jax.nn.log_sigmoid(z)
        log_1m_beta = jnp.where(causal, log_beta - z, 0.0)
        tail = lax.cumsum(log_1m_beta, axis=3, reverse=True) - log_1m_beta
        w = jnp.where(causal, jnp.exp(log_beta + tail), 0.0)
        outs.append(jnp.einsum('bhts,bhsd->bhtd', w.astype(v.dtype), v[:, :, :q1]))
    return jnp.concatenate(outs, axis=2)

def gla_chunked(q, k, v, log_a):
    b_, h_, s_len, dk = q.shape
    dv = v.shape[-1]
    c = GLA_CHUNK
    n = s_len // c
    qf = q.astype(jnp.float32).reshape(b_, h_, n, c, dk) * (dk ** -0.5)
    kf = k.astype(jnp.float32).reshape(b_, h_, n, c, dk)
    vf = v.astype(jnp.float32).reshape(b_, h_, n, c, dv)
    cum = jnp.cumsum(log_a.astype(jnp.float32).reshape(b_, h_, n, c, dk), axis=3)
    cum_last = cum[:, :, :, -1:, :]
    q_dec = qf * jnp.exp(cum)
    k_inv = kf * jnp.exp(-cum)
    k_end = kf * jnp.exp(cum_last - cum)
    tri = jnp.tril(jnp.ones((c, c), dtype=bool))
    scores = jnp.where(tri, jnp.einsum('bhnid,bhnjd->bhnij', q_dec, k_inv), 0.0)
    o_intra = jnp.einsum('bhnij,bhnjv->bhniv', scores, vf)
    kv_chunk = jnp.einsum('bhnjd,bhnjv->bhndv', k_end, vf)
    decay_chunk = jnp.exp(cum_last[:, :, :, 0, :])

    def step(state, inp):
        dec, kv = inp
        return dec[..., None] * state + kv, state

    _, states = lax.scan(step, jnp.zeros((b_, h_, dk, dv), jnp.float32),
                         (jnp.moveaxis(decay_chunk, 2, 0), jnp.moveaxis(kv_chunk, 2, 0)))
    states = jnp.moveaxis(states, 0, 2)
    o_inter = jnp.einsum('bhnid,bhndv->bhniv', q_dec, states)
    return (o_intra + o_inter).reshape(b_, h_, s_len, dv).astype(v.dtype)

def memory_cross_attention(q, mk, mv):
    d = q.shape[-1]
    s = jnp.einsum('bhtd,bhmd->bhtm', q.astype(jnp.float32), mk.astype(jnp.float32)) * (d ** -0.5)
    p = jax.nn.softmax(s, axis=-1)
    return jnp.einsum('bhtm,bhmd->bhtd', p.astype(mv.dtype), mv)

def hybrid_mixer(x, mem, norm_g, w_in, sb_q_g, sb_k_g, gla_a_up, gla_a_b, gla_o_g, ca_q_g, ca_k_g,
                 mem_norm_g, w_mem_kv, w_br_sb, w_br_gla, w_br_ca, w_out):
    b_, s_len, dm = x.shape
    h = rms_norm(x, norm_g)
    proj = h @ w_in
    offsets = np.cumsum(IN_SPLITS)[:-1].tolist()
    sb_q, sb_k, sb_v, g_q, g_k, g_v, g_a, g_r, ca_q, gates = jnp.split(proj, offsets, axis=-1)

    q_a = rms_norm(split_heads(sb_q, SB_HEADS), sb_q_g)
    k_a = rms_norm(split_heads(sb_k, SB_HEADS), sb_k_g)
    o_a = merge_heads(stick_breaking_attention(q_a, k_a, split_heads(sb_v, SB_HEADS)))

    log_a = jax.nn.log_sigmoid((g_a @ gla_a_up + gla_a_b).astype(jnp.float32)) / GLA_GATE_TAU
    o_b = gla_chunked(split_heads(g_q, GLA_HEADS), split_heads(g_k, GLA_HEADS),
                      split_heads(g_v, GLA_HEADS), split_heads(log_a, GLA_HEADS))
    o_b = merge_heads(rms_norm(o_b, gla_o_g)) * jax.nn.silu(g_r)

    mkv = rms_norm(mem, mem_norm_g) @ w_mem_kv
    m_k, m_v = jnp.split(mkv, 2, axis=-1)
    q_c = rms_norm(split_heads(ca_q, CA_HEADS), ca_q_g)
    k_c = rms_norm(split_heads(m_k, CA_HEADS), ca_k_g)
    o_c = merge_heads(memory_cross_attention(q_c, k_c, split_heads(m_v, CA_HEADS)))

    g = jax.nn.sigmoid(gates.astype(jnp.float32)).astype(x.dtype).reshape(b_, s_len, N_BRANCH, dm)
    merged = g[:, :, 0] * (o_a @ w_br_sb) + g[:, :, 1] * (o_b @ w_br_gla) + g[:, :, 2] * (o_c @ w_br_ca)
    return merged @ w_out

def swiglu(h, w_gate_up, w_down):
    gt, up = jnp.split(h @ w_gate_up, 2, axis=-1)
    return (jax.nn.silu(gt) * up) @ w_down

def moe_swiglu(h, w_router, w_gate_up, w_down):
    b_, s_len, dm = h.shape
    t = h.reshape(-1, dm)
    logits = (t @ w_router).astype(jnp.float32)
    top_val, top_idx = lax.top_k(logits, TOP_K)
    top_w = jax.nn.softmax(top_val, axis=-1)
    combine = jnp.sum(jax.nn.one_hot(top_idx, N_EXPERTS, dtype=jnp.float32) * top_w[..., None], axis=1)
    combine = combine.astype(t.dtype)
    y = jnp.zeros_like(t)
    for e in range(N_EXPERTS):
        y = y + combine[:, e:e + 1] * swiglu(t, w_gate_up[e], w_down[e])
    return y.reshape(b_, s_len, dm)

def setup_inputs(seed: int = 0) -> dict:
    key = jax.random.key(seed)
    ks = jax.random.split(key, 24)
    f32 = jnp.float32
    L = DEPTH

    def nrm(k, shape, fan_in):
        return jax.random.normal(k, shape, f32) * (fan_in ** -0.5)

    def gain(k, shape):
        return 1.0 + 0.1 * jax.random.normal(k, shape, f32)

    return {
        'x': jax.random.normal(ks[0], (BATCH, SEQ, D_MODEL), f32),
        'mem': jax.random.normal(ks[1], (BATCH, MEM_LEN, D_MODEL), f32),
        'mix_norm_g': gain(ks[2], (L, D_MODEL)),
        'w_in': nrm(ks[3], (L, D_MODEL, IN_WIDTH), D_MODEL),
        'sb_q_g': gain(ks[4], (L, SB_HEAD_DIM)),
        'sb_k_g': gain(ks[5], (L, SB_HEAD_DIM)),
        'gla_a_up': nrm(ks[6], (L, GLA_GATE_RANK, GLA_KW), GLA_GATE_RANK),
        'gla_a_b': 0.1 * jax.random.normal(ks[7], (L, GLA_KW), f32),
        'gla_o_g': gain(ks[8], (L, GLA_DV)),
        'ca_q_g': gain(ks[9], (L, CA_HEAD_DIM)),
        'ca_k_g': gain(ks[10], (L, CA_HEAD_DIM)),
        'mem_norm_g': gain(ks[11], (L, D_MODEL)),
        'w_mem_kv': nrm(ks[12], (L, D_MODEL, 2 * CA_WIDTH), D_MODEL),
        'w_br_sb': nrm(ks[13], (L, SB_WIDTH, D_MODEL), SB_WIDTH),
        'w_br_gla': nrm(ks[14], (L, GLA_VW, D_MODEL), GLA_VW),
        'w_br_ca': nrm(ks[15], (L, CA_WIDTH, D_MODEL), CA_WIDTH),
        'w_out': nrm(ks[16], (L, D_MODEL, D_MODEL), D_MODEL),
        'ffn_norm_g': gain(ks[17], (L, D_MODEL)),
        'ff_w_gate_up': nrm(ks[18], (N_DENSE, D_MODEL, 2 * D_FF), D_MODEL),
        'ff_w_down': nrm(ks[19], (N_DENSE, D_FF, D_MODEL), D_FF),
        'moe_w_router': nrm(ks[20], (N_MOE, D_MODEL, N_EXPERTS), D_MODEL),
        'moe_w_gate_up': nrm(ks[21], (N_MOE, N_EXPERTS, D_MODEL, 2 * D_FF_EXPERT), D_MODEL),
        'moe_w_down': nrm(ks[22], (N_MOE, N_EXPERTS, D_FF_EXPERT, D_MODEL), D_FF_EXPERT),
    }

def reference(x, mem, mix_norm_g, w_in, sb_q_g, sb_k_g, gla_a_up, gla_a_b, gla_o_g, ca_q_g, ca_k_g,
              mem_norm_g, w_mem_kv, w_br_sb, w_br_gla, w_br_ca, w_out, ffn_norm_g,
              ff_w_gate_up, ff_w_down, moe_w_router, moe_w_gate_up, moe_w_down):
    for layer in range(DEPTH):
        x = x + hybrid_mixer(x, mem, mix_norm_g[layer], w_in[layer], sb_q_g[layer], sb_k_g[layer],
                             gla_a_up[layer], gla_a_b[layer], gla_o_g[layer], ca_q_g[layer], ca_k_g[layer],
                             mem_norm_g[layer], w_mem_kv[layer], w_br_sb[layer], w_br_gla[layer],
                             w_br_ca[layer], w_out[layer])
        h = rms_norm(x, ffn_norm_g[layer])
        j = layer // 2
        if layer % 2 == 0:
            x = x + swiglu(h, ff_w_gate_up[j], ff_w_down[j])
        else:
            x = x + moe_swiglu(h, moe_w_router[j], moe_w_gate_up[j], moe_w_down[j])
    return x


_drawn_inputs = setup_inputs


def setup_inputs(seed=0):
    import zlib

    import numpy as np

    out = dict(_drawn_inputs(seed))
    spreads = {}
    factors = {'ca_q_g': 2.844}
    for name, (base, spread) in spreads.items():
        noise = np.random.default_rng([zlib.crc32(name.encode()), seed]).standard_normal(out[name].shape)
        drawn = base * np.exp(spread * noise) if base else spread * noise
        out[name] = __import__('jax').numpy.asarray(drawn.astype(out[name].dtype))
    for name, factor in factors.items():
        out[name] = (out[name] * factor).astype(out[name].dtype)
    return out
```

```python
from contextlib import ExitStack

import concourse.bass as bass
from concourse import mybir

F32 = mybir.dt.float32
F32R = mybir.dt.float32r
I32 = mybir.dt.int32
U32 = mybir.dt.uint32
ALU = mybir.AluOpType
ACT = mybir.ActivationFunctionType
AX = mybir.AxisListType

P = 128
SEQ, DM, MEM = 256, 1024, 256
NT = SEQ // P
KT = DM // P
LAYERS = 2
EPS = 1e-6
BW = 512
SB_HEADS, SB_DH = 8, 64
GLA_HEADS, GLA_DK, GLA_DV, GLA_CHUNK, GATE_RANK, GATE_TAU = 4, 64, 128, 64, 16, 16.0
CA_HEADS, CA_DH = 4, 128
BRANCHES = 3
D_FF, EXPERTS, D_EXP = 2816, 8, 3584

C_SBQ, C_SBK, C_SBV, C_GQK, C_GV = 0, BW, 2 * BW, 3 * BW, 4 * BW
C_GA = C_GV + GLA_HEADS * GLA_DV
C_GR = C_GA + GATE_RANK
C_CAQ = C_GR + GLA_HEADS * GLA_DV
C_GATE = C_CAQ + CA_HEADS * CA_DH

SLAB = 1024
RAW, SPLIT = 7, 4
AHEAD = 3

FF_BLOCKS = [(c, min(BW, D_FF - c)) for c in range(0, D_FF, BW)]
FF_PARTS = [FF_BLOCKS[:3], FF_BLOCKS[3:]]
FF_KT = 3 * BW // P

STEPS = D_EXP // BW
HT = BW // P
GU = KT * BW // SLAB
EXP_SLABS = STEPS * (2 * GU + HT)
CAP = P
OVER = 3
SLOTS = EXPERTS + OVER
BIAS = 32
GAINS = 16 * LAYERS * 9


class Product:

    def __init__(self, name, layer, kind, lhs, slabs, width, banks, taker):
        self.name, self.layer, self.kind, self.lhs = name, layer, kind, lhs
        self.slabs, self.width, self.banks, self.taker = slabs, width, banks, taker


def product_table(w_in, w_mem_kv, w_br, w_out, ff_gu, ff_down, w_router):
    table = []

    def add(name, layer, kind, lhs, slabs, width, banks, taker):
        p = Product(name, layer, kind, lhs, slabs, width, banks, taker)
        p.first = sum(len(q.slabs) for q in table)
        p.end = p.first + len(slabs)
        p.before = [q for q in table if q.banks & banks][-3:]
        p.nth = sum(q.taker == taker for q in table) + 1
        table.append(p)

    pairs = [frozenset((0, 1)), frozenset((2, 3))]
    four, side = frozenset(range(4)), frozenset(range(4, 8))
    turn = [0]

    def cols(name, layer, w, c, width, lhs, taker, pair=None):
        if pair is None:
            pair = turn[0] % 2
            turn[0] += 1
        v = w.rearrange("(k p) n -> p k n", p=P)[:, :, c:c + width]
        if width < 256:
            slabs = [v]
        else:
            n = SLAB // width
            slabs = [v[:, k:k + n, :] for k in range(0, KT, n)]
        add(name, layer, "cols", lhs, slabs, width, pairs[pair], taker)

    def rows(name, layer, w, r, n, lhs, banks):
        slabs = [w[r + P * k:r + P * (k + 1), :] for k in range(n)]
        add(name, layer, "rows", lhs, slabs, DM, banks, "dve")

    for l in range(LAYERS):
        cols("mem_k", l, w_mem_kv[l], 0, BW, "xt0", "act")
        cols("mem_v", l, w_mem_kv[l], BW, BW, "xt0", "act")
        for name, c, width in (("sb_q", C_SBQ, BW), ("sb_k", C_SBK, BW), ("sb_v", C_SBV, BW),
                               ("gla_qk", C_GQK, BW), ("ca_q", C_CAQ, BW), ("gla_v", C_GV, BW),
                               ("gla_a", C_GA, GATE_RANK), ("gla_r", C_GR, BW)):
            cols(name, l, w_in[l], c, width, "xt1", "act")
        for b in range(BRANCHES):
            for h in range(2):
                cols(f"gate{h}", l, w_in[l], C_GATE + b * DM + h * BW, BW, "xt1", "act")
            rows(f"branch{b}", l, w_br[b][l], 0, 4, f"ot{b % 2}", four)
        rows("out", l, w_out[l], 0, KT, "xt0", four)
        if l == 0:
            for part in FF_PARTS:
                for c, width in part:
                    cols("ff_gate", l, ff_gu, c, width, "xt0", "act", 0)
                    cols("ff_up", l, ff_gu, D_FF + c, width, "xt0", "dve", 1)
                rows("ff_down", l, ff_down, part[0][0], sum(x[1] for x in part) // P, "ht", side)
        else:
            cols("router", l, w_router, 0, EXPERTS, "xt0", "dve")
    return table


def trunk(nc, x_in, mem_in, mix_norm_g, w_in, sb_q_g, sb_k_g, gla_a_up, gla_a_b, gla_o_g, ca_q_g,
          ca_k_g, mem_norm_g, w_mem_kv, w_br_sb, w_br_gla, w_br_ca, w_out, ffn_norm_g, ff_gate_up,
          ff_down, moe_router, moe_gate_up, moe_down, out):
    table = product_table(w_in, w_mem_kv, (w_br_sb, w_br_gla, w_br_ca), w_out, ff_gate_up[0],
                          ff_down[0], moe_router[0])
    flat = [s for p in table for s in p.slabs]
    PRE = len(flat)
    tokens = x_in[0].rearrange("(t p) d -> p t d", p=P)
    memory_in = mem_in[0].rearrange("(t p) d -> p t d", p=P)
    result = out[0].rearrange("(t p) d -> p t d", p=P)

    with ExitStack() as ctx:
        def sb(name, shape, dt=F32):
            return ctx.enter_context(nc.sbuf_tensor(name, shape, dt))

        def sem(name):
            return ctx.enter_context(nc.semaphore(name))

        w_raw = sb("w_raw", [P, RAW, SLAB])
        w_hi = sb("w_hi", [P, SPLIT, SLAB], F32R)
        w_lo = sb("w_lo", [P, SPLIT, SLAB], F32R)
        xs = sb("xs", [P, NT, DM])
        hn = sb("hn", [P, NT, DM])
        gain = sb("gain", [P, DM])
        gates = sb("gates", [P, NT, DM])
        tok = sb("tok", [P, NT, BW])
        sq = sb("sq", [P, NT, BW])
        qT = sb("qT", [P, 4, SEQ])
        kT = sb("kT", [P, 4, SEQ])
        sv = sb("sv", [P, NT, BW])
        gqk = sb("gqk", [P, NT, BW])
        gv = sb("gv", [P, NT, BW])
        gr = sb("gr", [P, NT, BW])
        cqT = sb("cqT", [P, CA_HEADS, SEQ])
        ckT = sb("ckT", [P, CA_HEADS, MEM])
        cv = sb("cv", [P, NT, BW])
        scr = sb("scr", [P, 5120])
        head_gains = sb("head_gains", [P, LAYERS, 5])
        a_up = sb("a_up", [BIAS + 1, LAYERS, GLA_HEADS * GLA_DK])
        ga = sb("ga", [P, NT, GATE_RANK])
        gaT = sb("gaT", [BIAS + 1, SEQ])
        ms = sb("ms", [P, 8])
        rstd = sb("rstd", [P, 8])
        hms, hrs = sb("hms", [P, 16]), sb("hrs", [P, 16])
        half = sb("half", [P, 16])
        nms, nrstd = sb("nms", [P, NT]), sb("nrstd", [P, NT])
        ident = sb("ident", [P, P])
        neg_tri = sb("neg_tri", [P, P])
        neg_one = sb("neg_one", [P, P])
        cum_tri = sb("cum_tri", [P, P])
        rev_tri = sb("rev_tri", [P, P])
        xt0 = sb("xt0", [P, 2, KT, SEQ], F32R)
        r1 = sb("r1", [P, 8192], F32R)
        xt1 = r1[:, 0:4096].rearrange("p (s k t) -> p s k t", s=2, k=KT)
        ot = [r1[:, 4096 + 2048 * i:6144 + 2048 * i].rearrange("p (s k t) -> p s k t", s=2, k=4)
              for i in range(2)]
        ht = r1[:, 0:2 * FF_KT * SEQ].rearrange("p (s k t) -> p s k t", s=2, k=FF_KT)

        def view(a, *dims):
            n = 1
            for d in dims:
                n *= d
            v = scr[:, a:a + n]
            names = "abc"[:len(dims)]
            if len(dims) == 1:
                return v
            return v.rearrange(f"p ({' '.join(names)}) -> p {' '.join(names)}",
                               **{k: d for k, d in zip(names[1:], dims[1:])})

        sb_u, sb_w, sb_e = view(0, 2, 384), view(768, 2, 384), view(1536, 2, 384)
        la, lg = view(0, NT, 256), view(512, NT, 256)
        ecT, einvT = view(1024, 2, SEQ), view(1536, 2, SEQ)
        erev, kend = view(2048, NT, 256), view(2560, NT, 256)
        qdT, kiT = view(3072, 2, SEQ), view(3584, 2, SEQ)
        scT = view(4096, 8, P)
        state = view(1536, 3, 2, GLA_DV)
        go = view(0, NT, BW)
        probs = view(0, 8, MEM)
        pT = view(2048, NT, CA_HEADS, SEQ)
        th = xt0[:, :, :, :].rearrange("p s k t -> p (s k t)").rearrange(
            "p (s t d) -> p s t d", s=2, t=NT)
        xg = r1[:, 0:2048].rearrange("p (s k c) -> p s k c", s=2, k=KT)
        hts = [r1[:, 2048 + 1024 * i:3072 + 1024 * i].rearrange("p (s k c) -> p s k c", s=2, k=HT)
               for i in range(3)]
        ysp = r1[:, 5120:7168].rearrange("p (s d) -> p s d", s=2)
        sel = r1[:, 7168:7424].rearrange("p (t c) -> p t c", t=NT)
        selT = r1[:, 7424:7680]
        buf = [0, 1] * 3 + [2]
        hs, hb = tok[:, 0, :], sq[:, 0, :]
        utri, ones = neg_tri, neg_one
        iota_c = rev_tri
        small = view(0, 512)

        def sm(a, *dims):
            n = 1
            for d in dims:
                n *= d
            v = small[:, a:a + n]
            return v if len(dims) == 1 else v.rearrange("p (a b) -> p a b", b=dims[1])

        E = EXPERTS
        logit, top, pick1, pick2 = (sm(16 * i, NT, E) for i in range(4))
        assign, topi = sm(64, NT, E), sm(80, NT, E)
        iota_e = sm(96, E)
        w1, w2, wd = sm(104, NT), sm(106, NT), sm(108, NT)
        over, oidx, ozero = sm(112, E), sm(120, E), sm(128, E)
        slotf = sm(136, 1 + OVER)
        order = sm(140, OVER)
        mk, mtmp = sm(144, OVER, E), sm(168, OVER, E)
        slot_pos, slot_comb = sm(192, NT, SLOTS + 1), sm(216, NT, SLOTS + 1)
        slot_i = sb("slot_i", [1, 4], I32)
        topu = sb("topu", [P, NT, E], U32)

        pa = ctx.enter_context(nc.psum_tensor("pa", [P, 4 * BW], F32))
        ps = ctx.enter_context(nc.psum_tensor("ps", [P, 4 * BW], F32))

        raw_ready = [sem(f"raw_ready{i}") for i in range(RAW)]
        hi_ready, lo_ready, slab_used = sem("hi_ready"), sem("lo_ready"), sem("slab_used")
        taken = {"act": sem("act_took"), "dve": sem("dve_took")}
        side_ready, side_free = sem("side_ready"), sem("side_free")
        mem_loaded = [sem("mem_loaded"), sem("mem_reloaded")]
        x_loaded, gain_loaded, gains_loaded = (sem(n) for n in (
            "x_loaded", "gain_loaded", "gains_loaded"))
        consts = sem("consts")
        norm_sq, norm_ms, norm_rs, norm_done = (sem(f"norm_{n}") for n in ("sq", "ms", "rs", "done"))
        turn_ready, turn_hi, turn_lo = sem("turn_ready"), sem("turn_hi"), sem("turn_lo")
        head_ms, head_rs, head_scaled, head_done = (sem(f"head_{n}") for n in (
            "ms", "rs", "scaled", "done"))
        sb_sp, sb_uu, sb_um, sb_min, sb_exp, sb_wm, sb_hi = (sem(f"sb_{n}") for n in (
            "softplus", "u", "u_masked", "arg", "weight", "weight_masked", "hi"))
        gla_at, gla_lg, gla_la, gla_exp, gla_dec, gla_sc, gla_zero, gla_mask, gla_state, \
            gla_o, gla_scaled, gla_hi = (sem(f"gla_{n}") for n in (
                "aT", "lg", "la", "exp", "dec", "scores", "zero", "masked", "states", "o",
                "scaled", "hi"))
        ca_max, ca_exp, ca_rec, ca_scaled, ca_pt, ca_ptv, ca_hi = (sem(f"ca_{n}") for n in (
            "max", "exp", "rec", "scaled", "pT_act", "pT_dve", "hi"))
        branch_lo = sem("branch_lo")
        merge_step, residual = sem("merge_step"), sem("residual")
        ff_silu, ff_h, ff_hi, ff_lo = (sem(f"ff_{n}") for n in ("silu", "h", "hi", "lo"))
        act_step, dve_step, pool_step = sem("act_step"), sem("dve_step"), sem("pool_step")
        r_const, r_hi, r_lo, r_logit, r_assign, r_wd, r_table = (sem(f"route_{n}") for n in (
            "consts", "tokens_hi", "tokens_lo", "logits", "assigned", "weights", "table"))
        r_sel0 = sem("route_sel0")
        sel_ready, gathered, xg_hi, xg_lo, selt_turned, selt_ready = (sem(n) for n in (
            "sel_ready", "gathered", "xg_hi", "xg_lo", "selt_turned", "selt_ready"))
        y_cleared = sem("y_cleared")
        e_silu, e_h, e_turned, e_hi, e_lo, y_hi, y_lo, scattered, added = (sem(n) for n in (
            "e_silu", "e_h", "e_turned", "e_hi", "e_lo", "y_hi", "y_lo", "scattered", "added"))
        stored = sem("stored")

        def raw_slot(j):
            return w_raw[:, j % RAW, :]

        def raw_of(p, j, n):
            return raw_slot(j)[:, 0:n]

        sizes = []
        for p in table:
            for s in p.slabs:
                sizes.append(KT * p.width if p.width < 256 else SLAB)

        block = ctx.enter_context(nc.Block())

        def in_order(side_work, product, alone):
            waiting = []

            def side():
                while waiting:
                    try:
                        next(waiting[0][1])
                        return
                    except StopIteration:
                        waiting.pop(0)

            def finish(name=None):
                while waiting and (name is None or any(n == name for n, _ in waiting)):
                    side()

            alone["start"]()
            for p in table:
                if p.name == "mem_k":
                    finish()
                    alone["x_norm"](p.layer)
                elif p.name == "mem_v":
                    alone["x_turn"](p.layer)
                elif p.name in ("branch0", "branch1", "branch2"):
                    finish({"branch0": "sb", "branch1": "gla", "branch2": "ca"}[p.name])
                elif p.name == "out":
                    alone["merged"](p.layer)
                elif p is first_gate or p.name == "router":
                    finish()
                    alone["ffn_tokens"](p.layer)
                elif p.name == "ff_down":
                    finish()
                    if p is last_down:
                        waiting.append(("memory", alone["memory"](p.layer + 1)))
                product(p, side, finish)
                for name, work in side_work(p):
                    waiting.insert(0 if name == "head" else len(waiting), (name, work))
            finish()

        first_gate = [p for p in table if p.name == "ff_gate"][0]
        last_down = [p for p in table if p.name == "ff_down"][-1]

        def side_names(p):
            return {"mem_k": ["head"], "sb_q": ["head"], "sb_k": ["head"], "ca_q": ["head"],
                    "sb_v": ["sb"], "gla_r": ["gla", "ca"], "ff_up": ["ff"]}.get(p.name, [])

        NORMED = ("mem_k", "sb_q", "sb_k", "ca_q")

        def nth_of(name, l):
            return [p.nth for p in table if p.name == name and p.layer == l][0]

        def acts_before(p):
            return sum(q.taker == "act" for q in table[:table.index(p)])

        def head_number(p):
            return [q for q in table if q.name in NORMED].index(p) + 1

        def head_dim(p):
            return SB_DH if p.name in ("sb_q", "sb_k") else CA_DH

        def hidden_tile(p):
            c = [q for q in table if q.name == "ff_up"].index(p)
            part = [x for x in FF_PARTS if FF_BLOCKS[c] in x][0]
            return (FF_BLOCKS[c][0] - part[0][0]) // P

        @block.sync
        def _(sp):
            sp.dma_start(hn[:, :, :], memory_in).then_inc(mem_loaded[0], 16)
            sp.dma_start(xs[:, :, :], tokens).then_inc(x_loaded, 16)
            for s, src in enumerate(flat):
                if s >= RAW:
                    sp.wait_ge(lo_ready, s - RAW + 1)
                dst = raw_slot(s)[:, 0:sizes[s]]
                if len(src.shape) == 3:
                    dst = dst.rearrange("p (k n) -> p k n", k=src.shape[1])
                sp.dma_start(dst, src).then_inc(raw_ready[s % RAW], 16)

            def expert_slabs(e, i):
                gate_up = moe_gate_up[0].rearrange("e (k p) n -> e p k n", p=P)
                j = 0

                def load(src, k):
                    nonlocal j
                    slot = (PRE + j) % RAW
                    sp.wait_ge(lo_ready, i * EXP_SLABS + (PRE + j - RAW + 1))
                    dst = w_raw[:, slot, :]
                    if k > 1:
                        dst = dst.rearrange("p (k n) -> p k n", k=k)
                    sp.dma_start(dst, src).then_inc(raw_ready[slot], 16)
                    j += 1

                def cols(c):
                    n = SLAB // BW
                    for k in range(0, KT, n):
                        load(gate_up[bass.ds(e, 1), :, k:k + n, c:c + BW]
                             .rearrange("e p k n -> p (e k) n"), n)

                def rows(s):
                    for k in range(HT * s, HT * (s + 1)):
                        load(moe_down[0][bass.ds(e, 1), P * k:P * (k + 1), :]
                             .rearrange("e p n -> p (e n)"), 1)

                for s in range(STEPS):
                    cols(BW * s)
                    cols(D_EXP + BW * s)
                    if s > 0:
                        rows(s - 1)
                rows(STEPS - 1)

            with sp.Fori(0, EXPERTS) as e:
                expert_slabs(e, e)
            sp.wait_ge(r_table, 1)
            slots = sp.value_load(slot_i[0:1, 0:1], min_val=EXPERTS, max_val=SLOTS)
            with sp.If(slots > EXPERTS) as _:
                with sp.Fori(EXPERTS, slots) as i:
                    e = sp.value_load(slot_i[0:1, bass.ds(i - (EXPERTS - 1), 1)], min_val=0,
                                      max_val=EXPERTS - 1)
                    expert_slabs(e, i)
            sp.wait_ge(added, slots * NT + NT)
            sp.dma_start(result, xs[:, :, :]).then_inc(stored, 16)
            sp.wait_ge(stored, 16)

        @block.gpsimd
        def _(pool):
            steps = 0

            def link(ins):
                nonlocal steps
                steps += 1
                ins.then_inc(pool_step, 1)
                pool.wait_ge(pool_step, steps)

            gain_order = [g[l] for l in range(LAYERS) for g in (mem_norm_g, mix_norm_g, ffn_norm_g)]

            def load_gain(k):
                if k > 0:
                    pool.wait_ge(norm_done, NT * k)
                pool.dma_start(gain[:, :], gain_order[k].rearrange("(o d) -> o d", o=1)
                               .broadcast_to([P, DM])).then_inc(gain_loaded, 16)

            def start():
                load_gain(0)
                link(pool.memset(half[:, :], -0.5))
                link(pool.memset(ident[:, :], 0.0))
                pool.affine_select(out=ident[:, :], in_=ident[:, :], compare_op=ALU.not_equal,
                                   fill=1.0, base=0, pattern=[[-1, P]], channel_multiplier=1)\
                    .then_inc(consts, 1)
                pool.wait_ge(consts, 1)
                inverse_root()
                load_gain(1)
                link(pool.memset(a_up[:, :, :], 0.0))
                for l in range(LAYERS):
                    for i, (g, n) in enumerate(((sb_q_g, SB_DH), (sb_k_g, SB_DH), (gla_o_g, GLA_DV),
                                                (ca_q_g, CA_DH), (ca_k_g, CA_DH))):
                        for r in range(0, P, n):
                            pool.dma_start(head_gains[r:r + n, l, i:i + 1],
                                           g[l].rearrange("(d o) -> d o", o=1),
                                           allow_slow_non_contiguous=True).then_inc(gains_loaded, 16)
                    pool.dma_start(a_up[0:GATE_RANK, l, :], gla_a_up[l]).then_inc(gains_loaded, 16)
                    pool.dma_start(a_up[BIAS:BIAS + 1, l, :], gla_a_b[l]
                                   .rearrange("(o d) -> o d", o=1)).then_inc(gains_loaded, 16)
                link(pool.memset(gaT[:, :], 0.0))
                link(pool.memset(gaT[BIAS:BIAS + 1, :], 1.0))
                link(pool.memset(neg_tri[:, :], -1.0))
                link(pool.memset(neg_one[:, :], -1.0))
                link(pool.memset(cum_tri[:, :], 1.0 / GATE_TAU))
                link(pool.memset(rev_tri[:, :], 1.0 / GATE_TAU))
                link(pool.affine_select(out=neg_tri[:, :], in_=neg_tri[:, :], compare_op=ALU.is_ge,
                                        fill=0.0, base=0, pattern=[[-1, P]], channel_multiplier=1))
                link(pool.affine_select(out=cum_tri[:, :], in_=cum_tri[:, :], compare_op=ALU.is_ge,
                                        fill=0.0, base=0, pattern=[[1, P]], channel_multiplier=-1))
                link(pool.affine_select(out=rev_tri[:, :], in_=rev_tri[:, :], compare_op=ALU.is_gt,
                                        fill=0.0, base=0, pattern=[[-1, P]], channel_multiplier=1))
                link(pool.memset(cum_tri[0:GLA_CHUNK, GLA_CHUNK:P], 0.0))
                pool.memset(rev_tri[GLA_CHUNK:P, 0:GLA_CHUNK], 0.0).then_inc(consts, 1)
                pool.wait_ge(consts, 2)

            norms = 0

            def inverse_root():
                nonlocal norms
                pool.wait_ge(norm_ms, norms + 1)
                pool.tensor_tensor(nrstd[:, :], nms[:, :], half[:, 0:NT], ALU.pow)\
                    .then_inc(norm_rs, 1)
                norms += 1
                pool.wait_ge(norm_rs, norms)

            def memory(l):
                inverse_root()
                load_gain(3 * l + 1)
                yield
                yield

            def x_norm(l):
                inverse_root()
                load_gain(3 * l + 2)

            def x_turn(l):
                pass

            def merged(l):
                pass

            def ffn_norm(l):
                inverse_root()
                if l + 1 < LAYERS:
                    load_gain(3 * l + 3)
                    pool.wait_ge(turn_ready, 4 * (l + 1))
                    pool.dma_start(hn[:, :, :], memory_in).then_inc(mem_loaded[l + 1], 16)

            def product(p, side, finish):
                for s in range(p.first, p.end):
                    side()
                if p.name in NORMED:
                    finish("head")
                    head_norm(NT * BW // head_dim(p), hrs, hms)

            heads = 0

            def head_norm(n, dst, src):
                nonlocal heads
                heads += 1
                pool.wait_ge(head_ms, heads)
                pool.tensor_tensor(dst[:, 0:n], src[:, 0:n], half[:, 0:n], ALU.pow)\
                    .then_inc(head_rs, 1)
                pool.wait_ge(head_rs, heads)

            def head_work():
                yield
                yield

            def sb_work(l):
                for c in range(SB_HEADS // 2):
                    k = 4 * l + c
                    pool.wait_ge(sb_uu, k + 1)
                    link(pool.affine_select(out=sb_u[:, :, 0:P], in_=sb_u[:, :, 0:P],
                                            compare_op=ALU.is_gt, fill=0.0, base=0,
                                            pattern=[[0, 2], [1, P]], channel_multiplier=-1))
                    pool.affine_select(out=sb_u[:, :, SEQ:SEQ + P], in_=sb_u[:, :, SEQ:SEQ + P],
                                       compare_op=ALU.is_gt, fill=0.0, base=0,
                                       pattern=[[0, 2], [1, P]], channel_multiplier=-1)\
                        .then_inc(sb_um, 1)
                    pool.wait_ge(sb_um, k + 1)
                    yield
                    yield
                    pool.wait_ge(sb_exp, k + 1)
                    link(pool.affine_select(out=sb_w[:, :, 0:P], in_=sb_w[:, :, 0:P],
                                            compare_op=ALU.is_gt, fill=0.0, base=0,
                                            pattern=[[0, 2], [1, P]], channel_multiplier=-1))
                    pool.affine_select(out=sb_w[:, :, SEQ:SEQ + P], in_=sb_w[:, :, SEQ:SEQ + P],
                                       compare_op=ALU.is_gt, fill=0.0, base=0,
                                       pattern=[[0, 2], [1, P]], channel_multiplier=-1)\
                        .then_inc(sb_wm, 1)
                    pool.wait_ge(sb_wm, k + 1)
                    yield
                    yield
                    yield

            def gla_work(l):
                yield
                yield
                yield
                yield
                pool.wait_ge(gla_la, l + 1)
                pool.memset(scT, 0.0).then_inc(gla_zero, 1)
                pool.wait_ge(gla_zero, l + 1)
                yield
                pool.wait_ge(gla_sc, l + 1)
                pool.affine_select(out=scT, in_=scT, compare_op=ALU.is_ge, fill=0.0, base=0,
                                   pattern=[[0, 8], [1, P]], channel_multiplier=-1)\
                    .then_inc(gla_mask, 1)
                pool.wait_ge(gla_mask, l + 1)
                yield
                yield
                head_norm(NT * GLA_HEADS, rstd, ms)
                yield
                yield
                yield

            def ca_work(l):
                for _ in range(7):
                    yield

            def ff_work():
                yield

            def side_work(p):
                l = p.layer
                for name in side_names(p):
                    yield name, (head_work() if name == "head" else sb_work(l) if name == "sb"
                                 else gla_work(l) if name == "gla" else ca_work(l) if name == "ca"
                                 else ff_work())

            in_order(side_work, product, {"start": start, "memory": memory, "x_norm": x_norm,
                                          "x_turn": x_turn, "merged": merged,
                                          "ffn_tokens": ffn_norm})

            pool.wait_ge(turn_ready, 4 * LAYERS)
            link(pool.memset(ones[:, :], 1.0))
            link(pool.memset(utri[:, :], 1.0))
            link(pool.affine_select(out=utri[:, :], in_=utri[:, :], compare_op=ALU.is_gt, fill=0.0,
                                    base=0, pattern=[[1, P]], channel_multiplier=-1))
            link(pool.iota(iota_c[:, :], pattern=[[1, P]], base=0, channel_multiplier=0,
                           allow_small_or_imprecise_dtypes=True))
            link(pool.iota(order, pattern=[[1, OVER]], base=1, channel_multiplier=0,
                           allow_small_or_imprecise_dtypes=True))
            pool.iota(iota_e, pattern=[[1, E]], base=0, channel_multiplier=0,
                      allow_small_or_imprecise_dtypes=True).then_inc(r_const, 1)

        @block.scalar
        def _(act):
            steps = 0

            def link(ins):
                nonlocal steps
                steps += 1
                ins.then_inc(act_step, 1)
                act.wait_ge(act_step, steps)

            def split(s):
                act.wait_ge(raw_ready[s % RAW], 16 * (s // RAW + 1))
                if s >= SPLIT:
                    act.wait_ge(slab_used, s - SPLIT + 1)
                n = sizes[s]
                act.activation(w_hi[:, s % SPLIT, 0:n], raw_slot(s)[:, 0:n], ACT.Copy)\
                    .then_inc(hi_ready, 1)

            done = 0

            def splits_until(n):
                nonlocal done
                while done < min(n, PRE):
                    split(done)
                    done += 1

            visits = 0

            def visit():
                nonlocal visits
                visits += 1
                act.wait_ge(side_ready, visits)
                return visits

            norms = 0

            def norm(src):
                nonlocal norms
                for t in range(NT):
                    ins = act.activation(gates[:, t, :], src[:, t, :], ACT.Square,
                                         accum_out=nms[:, t:t + 1])
                    ins.then_inc(norm_sq, 1)
                norms += 1

            turns = 0

            def turned(dst, banks):
                nonlocal turns
                turns += 1
                act.wait_ge(turn_ready, turns)
                for t in range(NT):
                    act.activation(dst[:, 0, :, t * P:(t + 1) * P],
                                   banks[:, t * DM:(t + 1) * DM].rearrange("p (k t) -> p k t", k=KT),
                                   ACT.Copy).then_inc(turn_hi, 1)

            def start():
                for _ in memory(0):
                    pass

            def memory(l):
                act.wait_ge(mem_loaded[l], 16)
                norm(hn)
                yield
                turned(xt0, pa)
                yield

            def x_norm(l):
                if l == 0:
                    act.wait_ge(x_loaded, 16)
                else:
                    act.wait_ge(residual, 1 + len(FF_PARTS))
                norm(xs)

            def x_turn(l):
                turned(xt1, ps)

            def merged(l):
                turned(xt0, ps)

            def ffn_norm(l):
                act.wait_ge(residual, 1 if l == 0 else 2 + len(FF_PARTS))
                norm(xs)
                turned(xt0, ps)

            def bank(p, t):
                b = min(p.banks)
                return pa[:, (b + t) * BW:(b + t) * BW + p.width]

            gate_use = 0
            table_set = None

            def product(p, side, finish):
                nonlocal gate_use, table_set
                for s in range(p.first, p.end):
                    splits_until(s + 1 + AHEAD)
                    side()
                if p.name in NORMED:
                    finish("head")
                if p.taker != "act":
                    return
                act.wait_ge(slab_used, p.end)
                l = p.layer
                if p.name in NORMED:
                    for t in range(NT):
                        act.activation(tok[:, t, :], bank(p, t), ACT.Copy)
                        ins = act.activation(sq[:, t, :], bank(p, t), ACT.Square)
                    ins.then_inc(taken["act"], 1)
                    return
                dst, func = {"mem_v": (cv, ACT.Copy), "sb_v": (sv, ACT.Copy),
                             "gla_qk": (gqk, ACT.Copy), "gla_v": (gv, ACT.Copy),
                             "gla_a": (ga, ACT.Copy), "gla_r": (gr, ACT.Silu),
                             "gate0": (gates[:, :, 0:BW], ACT.Sigmoid),
                             "gate1": (gates[:, :, BW:DM], ACT.Sigmoid),
                             "ff_gate": (tok, ACT.Silu)}[p.name]
                if p.name == "gate0":
                    if gate_use % BRANCHES > 0:
                        act.wait_ge(merge_step, NT * gate_use)
                    gate_use += 1
                if p.name == "ff_gate" and blocks > 0:
                    act.wait_ge(ff_h, blocks)
                if func != ACT.Copy:
                    table_set = func
                for t in range(NT):
                    ins = act.activation(dst[:, t, 0:p.width], bank(p, t), func)
                ins.then_inc(taken["act"], 1)

            def head_work():
                yield
                visit()
                yield

            def exp_ln_table():
                nonlocal table_set
                if table_set != "natural_log_exp_and_others":
                    table_set = "natural_log_exp_and_others"
                    act.preload_act_table_set(table_set)

            def sb_work(l):
                for c in range(SB_HEADS // 2):
                    k = 4 * l + c
                    exp_ln_table()
                    visit()
                    z = ps[:, 0:2 * BW].rearrange("p (h n) -> p h n", h=2)[:, :, 0:384]
                    link(act.activation(sb_e, z, ACT.Abs))
                    link(act.activation(sb_e, sb_e, ACT.Exp, scale=-1.0))
                    act.activation(sb_e, sb_e, ACT.Ln, bias=1.0).then_inc(sb_sp, 1)
                    yield
                    yield
                    exp_ln_table()
                    visit()
                    act.wait_ge(sb_min, k + 1)
                    act.activation(sb_w, sb_w, ACT.Exp).then_inc(sb_exp, 1)
                    yield
                    yield
                    visit()
                    act.activation(ot[0][:, 0, c, :], ps[:, 0:SEQ], ACT.Copy).then_inc(sb_hi, 1)
                    yield

            def gla_work(l):
                visit()
                act.activation(gaT[0:GATE_RANK, :], ps[0:GATE_RANK, 0:SEQ], ACT.Copy).then_inc(gla_at, 1)
                yield
                exp_ln_table()
                visit()
                link(act.activation(lg.rearrange("p a b -> p (a b)"), ps[:, 0:BW], ACT.Abs))
                link(act.activation(lg, lg, ACT.Exp, scale=-1.0))
                act.activation(lg, lg, ACT.Ln, bias=1.0).then_inc(gla_lg, 1)
                yield
                yield
                exp_ln_table()
                visit()
                act.activation(ecT.rearrange("p a b -> p (a b)"), ps[:, 0:BW], ACT.Exp)
                act.activation(einvT.rearrange("p a b -> p (a b)"), ps[:, 0:BW], ACT.Exp, scale=-1.0)
                act.activation(erev.rearrange("p a b -> p (a b)"), ps[:, BW:2 * BW], ACT.Exp)\
                    .then_inc(gla_exp, 1)
                yield
                visit()
                yield
                visit()
                act.wait_ge(gla_zero, l + 1)
                for r in (0, GLA_CHUNK):
                    ins = act.activation(
                        scT[r:r + GLA_CHUNK, :, r:r + GLA_CHUNK],
                        ps[r:r + GLA_CHUNK, 2 * BW:4 * BW].rearrange("p (a i) -> p a i", a=8)
                        [:, :, r:r + GLA_CHUNK], ACT.Copy)
                ins.then_inc(gla_sc, 1)
                yield
                yield
                visit()
                for par in range(2):
                    src = ps[:, par * BW:(par + 1) * BW].rearrange("p (b t d) -> p t b d", b=2, t=NT)
                    for dst, func in ((go, ACT.Copy), (sq[:, :, :], ACT.Square)):
                        d = dst.rearrange("p t (b h d) -> p t b h d", b=2, h=2)[:, :, :, par, :]
                        ins = act.activation(d, src, func)
                ins.then_inc(gla_o, 1)
                yield
                yield
                visit()
                for t in range(NT):
                    act.activation(ot[1][:, 0, :, t * P:(t + 1) * P],
                                   ps[:, t * BW:(t + 1) * BW].rearrange("p (h t) -> p h t", h=4),
                                   ACT.Copy, scale=head_gains[:, l, 2:3]).then_inc(gla_hi, 1)
                yield

            def ca_work(l):
                exp_ln_table()
                visit()
                act.wait_ge(ca_max, l + 1)
                for a in range(NT * CA_HEADS):
                    ins = act.activation(probs[:, a, :], ps[:, a * MEM:(a + 1) * MEM], ACT.Exp,
                                         bias=ms[:, a:a + 1], scale=CA_DH ** -0.5,
                                         accum_out=rstd[:, a:a + 1])
                ins.then_inc(ca_exp, 1)
                yield
                yield
                yield
                yield
                visit()
                act.activation(pT[:, 0, :, :].rearrange("p h t -> p (h t)"), ps[:, 0:2 * BW],
                               ACT.Copy).then_inc(ca_pt, 1)
                yield
                yield
                visit()
                act.activation(ot[0][:, 0, :, :].rearrange("p h t -> p (h t)"), ps[:, 0:2 * BW],
                               ACT.Copy).then_inc(ca_hi, 1)
                yield

            blocks = 0

            def ff_work(width, k0):
                nonlocal blocks
                blocks += 1
                visit()
                n = width // P
                for t in range(NT):
                    act.activation(ht[:, 0, k0:k0 + n, t * P:(t + 1) * P],
                                   ps[:, t * BW:t * BW + width].rearrange("p (k t) -> p k t", k=n),
                                   ACT.Copy).then_inc(ff_hi, 1)
                yield

            def side_work(p):
                l = p.layer
                for name in side_names(p):
                    yield name, (head_work() if name == "head" else sb_work(l) if name == "sb"
                                 else gla_work(l) if name == "gla" else ca_work(l) if name == "ca"
                                 else ff_work(p.width, hidden_tile(p)))

            splits_until(AHEAD)
            in_order(side_work, product, {"start": start, "memory": memory, "x_norm": x_norm,
                                          "x_turn": x_turn, "merged": merged,
                                          "ffn_tokens": ffn_norm})

            act.preload_act_table_set("exp_and_others")
            act.wait_ge(slab_used, PRE)
            for t in range(NT):
                act.activation(th[:, 0, t, :], hn[:, t, :], ACT.Copy).then_inc(r_hi, 1)
            act.wait_ge(r_assign, 1)
            act.activation(wd, wd, ACT.Exp).then_inc(r_wd, 1)
            act.wait_ge(gathered, 1)
            act.activation(xg[:, 0, :, :].rearrange("p k c -> p (k c)"), ps[:, DM:2 * DM], ACT.Copy)\
                .then_inc(xg_hi, 1)
            act.preload_act_table_set("silu_and_others")

            act.wait_ge(r_table, 1)
            slots = act.value_load(slot_i[0:1, 0:1], min_val=EXPERTS, max_val=SLOTS)
            with act.Fori(0, slots) as i:
                at = i * EXP_SLABS
                j = 0

                def expert_split(n):
                    nonlocal j
                    while j < min(n, EXP_SLABS):
                        s = PRE + j
                        act.wait_ge(raw_ready[s % RAW], i * (16 * EXP_SLABS // RAW)
                                    + 16 * (s // RAW + 1))
                        act.wait_ge(slab_used, at + (s - SPLIT + 1))
                        act.activation(w_hi[:, s % SPLIT, :], raw_slot(s), ACT.Copy)\
                            .then_inc(hi_ready, 1)
                        j += 1

                expert_split(AHEAD)
                act.wait_ge(slab_used, at + PRE)
                act.wait_ge(y_cleared, 1)
                act.activation(ysp[:, 0, :], ps[:, 0:DM], ACT.Copy).then_inc(y_hi, 1)
                used = 0
                for s in range(STEPS + 1):
                    if s < STEPS:
                        for _ in range(GU):
                            used += 1
                            expert_split(used + AHEAD)
                        act.wait_ge(slab_used, at + (PRE + used))
                        if s > 0:
                            act.wait_ge(e_h, i * STEPS + s)
                        act.activation(hs, pa[:, 0:BW], ACT.Silu).then_inc(e_silu, 1)
                    if s == 0:
                        act.wait_ge(selt_turned, i + 1)
                        act.activation(selT, pa[:, 2 * BW:2 * BW + SEQ], ACT.Copy)\
                            .then_inc(selt_ready, 1)
                    else:
                        act.wait_ge(e_turned, i * STEPS + s)
                        act.activation(hts[buf[s - 1]][:, 0, :, :].rearrange("p k c -> p (k c)"),
                                       pa[:, 3 * BW:4 * BW], ACT.Copy).then_inc(e_hi, 1)
                    if s < STEPS:
                        for _ in range(GU):
                            used += 1
                            expert_split(used + AHEAD)
                    if s == STEPS - 1:
                        act.wait_ge(gathered, i * 2 + 3)
                        act.activation(xg[:, 0, :, :].rearrange("p k c -> p (k c)"),
                                       ps[:, DM:2 * DM], ACT.Copy).then_inc(xg_hi, 1)
                    if s > 0:
                        for _ in range(HT):
                            used += 1
                            expert_split(used + AHEAD)
            act.wait_ge(slab_used, slots * EXP_SLABS + PRE)
            act.activation(ysp[:, 0, :], ps[:, 0:DM], ACT.Copy).then_inc(y_hi, 1)

        @block.vector
        def _(dve):
            steps = 0

            def link(ins):
                nonlocal steps
                steps += 1
                ins.then_inc(dve_step, 1)
                dve.wait_ge(dve_step, steps)

            done = 0

            def splits_until(n):
                nonlocal done
                while done < min(n, PRE):
                    s, w = done, sizes[done]
                    dve.wait_ge(hi_ready, s + 1)
                    dve.tensor_tensor(w_lo[:, s % SPLIT, 0:w], raw_slot(s)[:, 0:w],
                                      w_hi[:, s % SPLIT, 0:w].bitcast(F32), ALU.subtract)\
                        .then_inc(lo_ready, 1)
                    done += 1

            visits = 0

            def visit():
                nonlocal visits
                visits += 1
                dve.wait_ge(side_ready, visits)

            norms = 0

            def norm(src):
                nonlocal norms
                dve.wait_ge(norm_sq, NT * (norms + 1))
                dve.tensor_scalar(nms[:, 0:NT], nms[:, 0:NT], 1.0 / DM, EPS, ALU.mult, ALU.add)\
                    .then_inc(norm_ms, 1)
                dve.wait_ge(norm_rs, norms + 1)
                dve.wait_ge(gain_loaded, 16 * (norms + 1))
                for t in range(NT):
                    dve.scalar_tensor_tensor(out=hn[:, t, :], in0=src[:, t, :],
                                             scalar=nrstd[:, t:t + 1], in1=gain[:, :], op0=ALU.mult,
                                             op1=ALU.mult).then_inc(norm_done, 1)
                norms += 1

            turns = 0

            def turned(dst, banks):
                nonlocal turns
                for t in range(NT):
                    turns += 1
                    dve.wait_ge(turn_hi, turns)
                    dve.tensor_tensor(
                        dst[:, 1, :, t * P:(t + 1) * P],
                        banks[:, t * DM:(t + 1) * DM].rearrange("p (k t) -> p k t", k=KT),
                        dst[:, 0, :, t * P:(t + 1) * P].bitcast(F32), ALU.subtract)\
                        .then_inc(turn_lo, 1)
                if banks is ps:
                    dve.wait_ge(turn_lo, turns)
                    dve.sem_inc(side_free, 1)

            def start():
                for _ in memory(0):
                    pass

            def memory(l):
                dve.wait_ge(mem_loaded[l], 16)
                norm(hn)
                yield
                turned(xt0, pa)
                yield

            def x_norm(l):
                if l == 0:
                    dve.wait_ge(x_loaded, 16)
                dve.wait_ge(turn_ready, turns // NT)
                norm(xs)

            def x_turn(l):
                turned(xt1, ps)
                if l == 0:
                    dve.wait_ge(gains_loaded, GAINS)

            def merged(l):
                turned(xt0, ps)

            def ffn_norm(l):
                norm(xs)
                turned(xt0, ps)

            def quad(p):
                return (pa if 0 in p.banks else ps)[:, :].rearrange("p (t d) -> p t d", t=NT)

            def product(p, side, finish):
                for s in range(p.first, p.end):
                    splits_until(s + 1 + AHEAD)
                    side()
                if p.name in NORMED:
                    finish("head")
                    dve.wait_ge(taken["act"], p.nth)
                    mean_squares(BW // head_dim(p), head_dim(p), hms)
                if p.taker != "dve":
                    return
                dve.wait_ge(slab_used, p.end)
                if p.name.startswith("branch"):
                    dve.wait_ge(taken["act"], acts_before(p))
                    b = int(p.name[-1])
                    for t in range(NT):
                        dst = hn if b == 0 else gates
                        ins = dve.tensor_tensor(dst[:, t, :], quad(p)[:, t, :], gates[:, t, :],
                                                ALU.mult)
                        if t == NT - 1:
                            ins.then_inc(taken["dve"], 1)
                            dve.wait_ge(taken["dve"], p.nth)
                        else:
                            link(ins)
                    for t in range(NT):
                        if b == 0:
                            dve.sem_inc(merge_step, 1)
                        else:
                            dve.tensor_tensor(hn[:, t, :], hn[:, t, :], gates[:, t, :], ALU.add)\
                                .then_inc(merge_step, 1)
                            dve.wait_ge(merge_step, NT * (BRANCHES * p.layer + b) + t + 1)
                elif p.name in ("out", "ff_down"):
                    for t in range(NT):
                        ins = dve.tensor_tensor(xs[:, t, :], quad(p)[:, t, :], xs[:, t, :], ALU.add)
                        if t == NT - 1:
                            ins.then_inc(taken["dve"], 1)
                            dve.wait_ge(taken["dve"], p.nth)
                        else:
                            link(ins)
                    dve.sem_inc(residual, 1)
                    if p.name == "ff_down":
                        dve.sem_inc(side_free, 1)
                elif p.name == "ff_up":
                    b = min(p.banks)
                    dve.wait_ge(taken["act"], acts_before(p))
                    for t in range(NT):
                        ins = dve.tensor_tensor(sq[:, t, 0:p.width],
                                                pa[:, (b + t) * BW:(b + t) * BW + p.width],
                                                tok[:, t, 0:p.width], ALU.mult)
                        if t == NT - 1:
                            ins.then_inc(taken["dve"], 1)
                            dve.wait_ge(taken["dve"], p.nth)
                        else:
                            link(ins)
                    dve.sem_inc(ff_h, 1)
                elif p.name == "router":
                    b = min(p.banks)
                    for t in range(NT):
                        ins = dve.tensor_copy(logit[:, t, :], pa[:, (b + t) * BW:(b + t) * BW + E])
                        if t == NT - 1:
                            ins.then_inc(taken["dve"], 1)
                            dve.wait_ge(taken["dve"], p.nth)
                        else:
                            link(ins)
                    dve.sem_inc(r_logit, 1)

            heads = 0

            def mean_squares(n, dh, ms):
                nonlocal heads
                heads += 1
                for t in range(NT):
                    ins = dve.tensor_reduce(ms[:, t * n:(t + 1) * n],
                                            sq[:, t, :].rearrange("p (h d) -> p h d", h=n),
                                            AX.X, ALU.add)
                    link(ins)
                dve.tensor_scalar(ms[:, 0:NT * n], ms[:, 0:NT * n], 1.0 / dh, EPS, ALU.mult,
                                  ALU.add).then_inc(head_ms, 1)

            def head_work(p):
                dh = head_dim(p)
                n = BW // dh
                dve.wait_ge(head_rs, heads)
                for t in range(NT):
                    v = tok[:, t, :].rearrange("p (h d) -> p h d", h=n)
                    ins = dve.tensor_tensor(v, v, hrs[:, t * n:(t + 1) * n].unsqueeze(2)
                                            .broadcast_to([P, n, dh]), ALU.mult)
                    ins.then_inc(head_scaled, 1)
                yield
                visit()
                dst, g, c = {"sb_q": (qT, 0, SB_DH ** -0.5), "sb_k": (kT, 1, 1.0),
                             "ca_q": (cqT, 3, 1.0), "mem_k": (ckT, 4, 1.0)}[p.name]
                for t in range(NT):
                    ins = dve.tensor_scalar(
                        dst[:, :, t * P:(t + 1) * P],
                        ps[:, t * BW:(t + 1) * BW].rearrange("p (a t) -> p a t", a=4),
                        head_gains[:, p.layer, g:g + 1], c, ALU.mult, ALU.mult)
                    if t == NT - 1:
                        ins.then_inc(head_done, 1)
                        dve.wait_ge(head_done, head_number(p))
                    else:
                        link(ins)
                dve.sem_inc(side_free, 1)
                yield

            def sb_work(l):
                for c in range(SB_HEADS // 2):
                    k = 4 * l + c
                    visit()
                    z = ps[:, 0:2 * BW].rearrange("p (h n) -> p h n", h=2)[:, :, 0:384]
                    dve.wait_ge(sb_sp, k + 1)
                    dve.scalar_tensor_tensor(out=sb_u, in0=z, scalar=0.0, in1=sb_e, op0=ALU.max,
                                             op1=ALU.add).then_inc(sb_uu, 1)
                    dve.wait_ge(sb_uu, k + 1)
                    dve.sem_inc(side_free, 1)
                    yield
                    yield
                    visit()
                    dve.tensor_scalar(sb_w, z, 0.0, None, ALU.min).then_inc(sb_min, 1)
                    dve.wait_ge(sb_min, k + 1)
                    dve.sem_inc(side_free, 1)
                    yield
                    yield
                    visit()
                    dve.wait_ge(sb_hi, k + 1)
                    link(dve.tensor_tensor(ot[0][:, 1, c, :], ps[:, 0:SEQ],
                                           ot[0][:, 0, c, :].bitcast(F32), ALU.subtract))
                    dve.sem_inc(side_free, 1)
                    yield
                dve.sem_inc(branch_lo, 1)

            def gla_work(l):
                visit()
                dve.wait_ge(gla_at, l + 1)
                dve.sem_inc(side_free, 1)
                yield
                visit()
                dve.wait_ge(gla_lg, l + 1)
                dve.scalar_tensor_tensor(out=la.rearrange("p a b -> p (a b)"), in0=ps[:, 0:BW],
                                         scalar=0.0, in1=lg.rearrange("p a b -> p (a b)"),
                                         op0=ALU.min, op1=ALU.subtract).then_inc(gla_la, 1)
                dve.wait_ge(gla_la, l + 1)
                dve.sem_inc(side_free, 1)
                yield
                yield
                visit()
                dve.wait_ge(gla_exp, l + 1)
                dve.sem_inc(side_free, 1)
                link(dve.tensor_tensor(kend, gqk[:, :, 256:512], erev, ALU.mult))
                yield
                visit()
                for t in range(NT):
                    v = ps[:, t * BW:(t + 1) * BW].rearrange("p (a b t) -> p a b t", a=2, b=2)
                    cols = slice(t * P, (t + 1) * P)
                    link(dve.scalar_tensor_tensor(out=qdT[:, :, cols], in0=v[:, 0], in1=ecT[:, :, cols],
                                                  scalar=GLA_DK ** -0.5, op0=ALU.mult, op1=ALU.mult))
                    link(dve.tensor_tensor(kiT[:, :, cols], v[:, 1], einvT[:, :, cols], ALU.mult))
                dve.sem_inc(gla_dec, 1)
                dve.sem_inc(side_free, 1)
                yield
                visit()
                for c in range(3):
                    kv = ps[:, (c % 2) * BW + (c // 2) * 256:(c % 2) * BW + (c // 2) * 256 + 256]\
                        .rearrange("p (b d) -> p b d", b=2)
                    if c == 0:
                        link(dve.tensor_copy(state[:, 0], kv))
                        continue
                    last = (c + 1) * GLA_CHUNK - 1
                    for b in range(2):
                        link(dve.scalar_tensor_tensor(
                            out=state[:, c, b, :], in0=state[:, c - 1, b, :],
                            scalar=ecT[:, b, last:last + 1], in1=kv[:, b, :], op0=ALU.mult,
                            op1=ALU.add))
                dve.sem_inc(gla_state, 1)
                dve.wait_ge(gla_sc, l + 1)
                dve.sem_inc(side_free, 1)
                yield
                yield
                visit()
                dve.wait_ge(gla_o, l + 1)
                dve.sem_inc(side_free, 1)
                mean_squares(GLA_HEADS, GLA_DV, ms)
                k = heads
                yield
                dve.wait_ge(head_rs, k)
                for t in range(NT):
                    v = go[:, t, :].rearrange("p (h d) -> p h d", h=GLA_HEADS)
                    link(dve.tensor_tensor(v, v, rstd[:, t * 4:(t + 1) * 4].unsqueeze(2)
                                           .broadcast_to([P, GLA_HEADS, GLA_DV]), ALU.mult))
                dve.tensor_tensor(go, go, gr[:, :, :], ALU.mult).then_inc(gla_scaled, 1)
                yield
                visit()
                for t in range(NT):
                    cols = slice(t * P, (t + 1) * P)
                    dve.wait_ge(gla_hi, NT * l + t + 1)
                    link(dve.scalar_tensor_tensor(
                        out=ot[1][:, 1, :, cols],
                        in0=ps[:, t * BW:(t + 1) * BW].rearrange("p (h t) -> p h t", h=4),
                        scalar=head_gains[:, l, 2:3], in1=ot[1][:, 0, :, cols].bitcast(F32),
                        op0=ALU.mult, op1=ALU.subtract))
                dve.sem_inc(side_free, 1)
                dve.sem_inc(branch_lo, 1)
                yield

            def ca_work(l):
                n = NT * CA_HEADS
                visit()
                link(dve.tensor_reduce(ms[:, 0:n], ps[:, :].rearrange("p (a m) -> p a m", a=n), AX.X,
                                       ALU.max))
                dve.tensor_scalar(ms[:, 0:n], ms[:, 0:n], -CA_DH ** -0.5, None, ALU.mult)\
                    .then_inc(ca_max, 1)
                yield
                yield
                dve.wait_ge(ca_exp, l + 1)
                dve.sem_inc(side_free, 1)
                link(dve.reciprocal(rstd[:, 0:n], rstd[:, 0:n]))
                yield
                dve.tensor_tensor(probs, probs, rstd[:, 0:n].unsqueeze(2).broadcast_to([P, n, MEM]),
                                  ALU.mult).then_inc(ca_scaled, 1)
                yield
                visit()
                dve.tensor_copy(pT[:, 1, :, :].rearrange("p h t -> p (h t)"), ps[:, 2 * BW:4 * BW])\
                    .then_inc(ca_ptv, 1)
                dve.wait_ge(ca_pt, l + 1)
                dve.wait_ge(ca_ptv, l + 1)
                dve.sem_inc(side_free, 1)
                yield
                yield
                visit()
                dve.wait_ge(ca_hi, l + 1)
                link(dve.tensor_tensor(ot[0][:, 1, :, :].rearrange("p h t -> p (h t)"),
                                       ps[:, 0:2 * BW],
                                       ot[0][:, 0, :, :].rearrange("p h t -> p (h t)").bitcast(F32),
                                       ALU.subtract))
                dve.sem_inc(side_free, 1)
                dve.sem_inc(branch_lo, 1)
                yield

            blocks = 0

            def ff_work(width, k0):
                nonlocal blocks
                blocks += 1
                visit()
                n = width // P
                for t in range(NT):
                    cols = slice(t * P, (t + 1) * P)
                    dve.wait_ge(ff_hi, NT * (blocks - 1) + t + 1)
                    ins = dve.tensor_tensor(
                        ht[:, 1, k0:k0 + n, cols],
                        ps[:, t * BW:t * BW + width].rearrange("p (k t) -> p k t", k=n),
                        ht[:, 0, k0:k0 + n, cols].bitcast(F32), ALU.subtract)
                    ins.then_inc(ff_lo, 1)
                dve.wait_ge(ff_lo, NT * blocks)
                dve.sem_inc(side_free, 1)
                yield

            def side_work(p):
                l = p.layer
                for name in side_names(p):
                    yield name, (head_work(p) if name == "head" else sb_work(l) if name == "sb"
                                 else gla_work(l) if name == "gla" else ca_work(l) if name == "ca"
                                 else ff_work(p.width, hidden_tile(p)))

            splits_until(AHEAD)
            in_order(side_work, product, {"start": start, "memory": memory, "x_norm": x_norm,
                                          "x_turn": x_turn, "merged": merged,
                                          "ffn_tokens": ffn_norm})

            dve.wait_ge(r_const, 1)
            for t in range(NT):
                link(dve.max(top[:, t, :], logit[:, t, :]))
                link(dve.max_index(topu[:, t, :], top[:, t, :], logit[:, t, :]))
            link(dve.tensor_copy(topi, topu[:, :, :]))
            every = iota_e.unsqueeze(1).broadcast_to([P, NT, E])
            link(dve.tensor_tensor(pick1, every, topi[:, :, 0:1].broadcast_to([P, NT, E]),
                                   ALU.is_equal))
            link(dve.tensor_tensor(pick2, every, topi[:, :, 1:2].broadcast_to([P, NT, E]),
                                   ALU.is_equal))
            link(dve.tensor_tensor(wd.unsqueeze(2), top[:, :, 1:2], top[:, :, 0:1], ALU.subtract))
            dve.tensor_tensor(assign, pick1, pick2, ALU.add).then_inc(r_assign, 1)
            link(dve.memset(slot_pos, -1.0))
            link(dve.memset(slot_comb, 0.0))
            link(dve.memset(ozero, 0.0))
            dve.memset(selT.bitcast(F32), 0.0).then_inc(selt_ready, 1)
            for t in range(NT):
                dve.wait_ge(r_hi, t + 1)
                dve.tensor_tensor(th[:, 1, t, :], hn[:, t, :], th[:, 0, t, :].bitcast(F32),
                                  ALU.subtract).then_inc(r_lo, 1)
            visit()
            pos = slot_pos[:, :, 0:E]
            link(dve.scalar_tensor_tensor(out=pos, in0=ps[:, 0:NT * E]
                                          .rearrange("p (t e) -> p t e", t=NT), scalar=1.0,
                                          in1=assign, op0=ALU.add, op1=ALU.mult))
            link(dve.tensor_scalar(pos, pos, 1.0, None, ALU.subtract))
            for t in range(NT):
                dve.tensor_scalar(sel[:, t, :], iota_c[:, :], slot_pos[:, t, 0:1], None,
                                  ALU.is_equal).then_inc(sel_ready, 1)
            link(dve.tensor_scalar(over, ps[:, NT * E:(NT + 1) * E], float(CAP), None, ALU.is_gt))
            link(dve.tensor_tensor_scan(oidx, over, ozero, 0.0, ALU.add, ALU.add))
            link(dve.tensor_scalar(slotf[:, 0:1], oidx[:, E - 1:E], float(E), None, ALU.add))
            three = [P, OVER, E]
            link(dve.tensor_tensor(mk, oidx.unsqueeze(1).broadcast_to(three),
                                   order.unsqueeze(2).broadcast_to(three), ALU.is_equal))
            link(dve.tensor_tensor(mk, mk, over.unsqueeze(1).broadcast_to(three), ALU.mult))
            link(dve.tensor_tensor(mtmp, mk, iota_e.unsqueeze(1).broadcast_to(three), ALU.mult))
            link(dve.tensor_reduce(slotf[:, 1:1 + OVER], mtmp, AX.X, ALU.add))
            dve.tensor_copy(slot_i[0:1, :], slotf[0:1, :]).then_inc(r_table, 1)
            dve.wait_ge(gathered, 2)
            dve.tensor_copy(xg[:, 1, :, :].rearrange("p k c -> p (k c)"), ps[:, DM:2 * DM])\
                .then_inc(xg_lo, 1)
            dve.wait_ge(r_wd, 1)
            link(dve.tensor_scalar(w1, wd, 1.0, None, ALU.add))
            link(dve.reciprocal(w1, w1))
            link(dve.tensor_tensor(w2, w1, wd, ALU.mult))
            link(dve.tensor_tensor(pick1, pick1, w1.unsqueeze(2).broadcast_to([P, NT, E]), ALU.mult))
            link(dve.tensor_tensor(pick2, pick2, w2.unsqueeze(2).broadcast_to([P, NT, E]), ALU.mult))
            comb = slot_comb[:, :, 1:1 + E]
            link(dve.tensor_tensor(comb, pick1, pick2, ALU.add))
            for t in range(NT):
                link(dve.tensor_tensor(mtmp, mk, pos[:, t:t + 1, :].broadcast_to(three), ALU.mult))
                link(dve.tensor_reduce(slot_pos[:, t, E:SLOTS], mtmp, AX.X, ALU.add))
                link(dve.tensor_scalar(slot_pos[:, t, E:SLOTS], slot_pos[:, t, E:SLOTS], float(CAP),
                                       None, ALU.subtract))
                link(dve.tensor_tensor(mtmp, mk, comb[:, t:t + 1, :].broadcast_to(three), ALU.mult))
                link(dve.tensor_reduce(slot_comb[:, t, 1 + E:1 + SLOTS], mtmp, AX.X, ALU.add))
            dve.memset(ps[:, 0:DM], 0.0).then_inc(y_cleared, 1)

            dve.wait_ge(r_table, 1)
            slots = dve.value_load(slot_i[0:1, 0:1], min_val=EXPERTS, max_val=SLOTS)

            def output_lo(n):
                dve.wait_ge(y_hi, n)
                dve.tensor_tensor(ysp[:, 1, :], ps[:, 0:DM], ysp[:, 0, :].bitcast(F32),
                                  ALU.subtract).then_inc(y_lo, 1)

            def add_slot(i):
                dve.wait_ge(scattered, i + 1)
                for t in range(NT):
                    q = (1 - t) * DM
                    dve.scalar_tensor_tensor(out=xs[:, t, :], in0=ps[:, q:q + DM],
                                             scalar=slot_comb[:, t, bass.ds(i, 1)],
                                             in1=xs[:, t, :], op0=ALU.mult, op1=ALU.add)\
                        .then_inc(added, 1)

            with dve.Fori(0, slots) as i:
                at = i * EXP_SLABS
                j = 0

                def expert_split(n):
                    nonlocal j
                    while j < min(n, EXP_SLABS):
                        s = PRE + j
                        dve.wait_ge(hi_ready, at + (s + 1))
                        dve.tensor_tensor(w_lo[:, s % SPLIT, :], raw_slot(s),
                                          w_hi[:, s % SPLIT, :].bitcast(F32), ALU.subtract)\
                            .then_inc(lo_ready, 1)
                        j += 1

                expert_split(AHEAD)
                output_lo(i + 1)
                used = 0
                for s in range(STEPS + 1):
                    if s < STEPS:
                        for _ in range(GU):
                            used += 1
                            expert_split(used + AHEAD)
                    if s > 0:
                        dve.wait_ge(e_hi, i * STEPS + s)
                        v = hts[buf[s - 1]][:, :, :, :].rearrange("p s k c -> p s (k c)")
                        dve.tensor_tensor(v[:, 1, :], pa[:, 3 * BW:4 * BW],
                                          v[:, 0, :].bitcast(F32), ALU.subtract).then_inc(e_lo, 1)
                    else:
                        add_slot(i)
                    if s < STEPS:
                        for _ in range(GU):
                            used += 1
                            expert_split(used + AHEAD)
                        dve.wait_ge(slab_used, at + (PRE + used))
                        dve.wait_ge(e_silu, i * STEPS + (s + 1))
                        if s > 0:
                            dve.wait_ge(e_turned, i * STEPS + s)
                        dve.tensor_tensor(hb, pa[:, BW:2 * BW], hs, ALU.mult).then_inc(e_h, 1)
                    if s == 1:
                        dve.wait_ge(selt_turned, i + 1)
                        for t in range(NT):
                            dve.tensor_scalar(sel[:, t, :], iota_c[:, :],
                                              slot_pos[:, t, bass.ds(i + 1, 1)], None,
                                              ALU.is_equal).then_inc(sel_ready, 1)
                    if s > 0:
                        for _ in range(HT):
                            used += 1
                            expert_split(used + AHEAD)
                    if s == STEPS - 1:
                        dve.wait_ge(gathered, i * 2 + 4)
                        dve.tensor_copy(xg[:, 1, :, :].rearrange("p k c -> p (k c)"),
                                        ps[:, DM:2 * DM]).then_inc(xg_lo, 1)
            output_lo(slots + 1)
            add_slot(slots)

        @block.tensor
        def _(pe):
            frees = 0

            def enter():
                nonlocal frees
                if frees:
                    pe.wait_ge(side_free, frees)
                frees += 1

            lhs_of = {"xt0": xt0, "xt1": xt1, "ot0": ot[0], "ot1": ot[1], "ht": ht}

            norms = turns = ffs = 0

            def turn_tokens(normed, banks):
                nonlocal norms, turns
                if normed:
                    norms += 1
                if banks is ps:
                    enter()
                for t in range(NT):
                    if normed:
                        pe.wait_ge(norm_done, NT * (norms - 1) + t + 1)
                    for k in range(KT):
                        ins = pe.transpose(banks[:, t * DM + k * P:t * DM + (k + 1) * P],
                                           hn[:, t, k * P:(k + 1) * P], ident[:, :])
                ins.then_inc(turn_ready, 1)
                turns += 1

            def start():
                pe.wait_ge(consts, 1)
                for _ in memory(0):
                    pass

            def memory(l):
                yield
                if l > 0:
                    last_up = [q for q in table if q.name == "ff_up"][-1]
                    pe.wait_ge(taken["dve"], last_up.nth)
                turn_tokens(True, pa)
                yield

            def x_norm(l):
                pass

            def x_turn(l):
                turn_tokens(True, ps)
                if l == 0:
                    pe.wait_ge(consts, 2)
                    pe.wait_ge(gains_loaded, GAINS)

            def merged(l):
                pe.wait_ge(merge_step, NT * BRANCHES * (l + 1))
                turn_tokens(False, ps)

            def ffn_norm(l):
                turn_tokens(True, ps)

            def passes(dst, hi, lo, m_hi, m_lo, first, last):
                pe.matmul(dst, hi, m_hi, start=first, stop=False)
                pe.matmul(dst, hi, m_lo, start=False, stop=False)
                return pe.matmul(dst, lo, m_hi, start=False, stop=last)

            def product(p, side, finish):
                for q in p.before:
                    pe.wait_ge(taken[q.taker], q.nth)
                if p.name == "ff_down":
                    enter()
                    pe.wait_ge(ff_lo, ffs * NT)
                if p.lhs in ("xt0", "xt1"):
                    pe.wait_ge(turn_lo, NT * turns)
                if p.name.startswith("branch"):
                    pe.wait_ge(branch_lo, BRANCHES * p.layer + int(p.name[-1]) + 1)
                lhs = lhs_of[p.lhs]
                b = min(p.banks)
                kts = len(p.slabs) * max(1, SLAB // p.width) if p.width >= 256 else KT
                per = kts // len(p.slabs)
                for n, s in enumerate(range(p.first, p.end)):
                    pe.wait_ge(lo_ready, s + 1)
                    for kk in range(per):
                        k = n * per + kk
                        for t in range(NT):
                            hi, lo = (lhs[:, h, k, t * P:(t + 1) * P] for h in range(2))
                            for c in range(0, p.width, BW):
                                w = min(BW, p.width - c)
                                at = kk * p.width + c
                                if p.kind == "cols":
                                    dst = pa[:, (b + t) * BW:(b + t) * BW + w]
                                else:
                                    dst = (pa if b == 0 else ps)[:, t * DM + c:t * DM + c + w]
                                ins = passes(dst, hi, lo, w_hi[:, s % SPLIT, at:at + w],
                                             w_lo[:, s % SPLIT, at:at + w], k == 0, k == kts - 1)
                    ins.then_inc(slab_used, 1)
                    side()
                if p.name in NORMED:
                    finish("head")

            headed = 0

            def head_work():
                nonlocal headed
                yield
                enter()
                for t in range(NT):
                    headed += 1
                    pe.wait_ge(head_scaled, headed)
                    for a in range(4):
                        ins = pe.transpose(ps[:, t * BW + a * P:t * BW + (a + 1) * P],
                                           tok[:, t, a * P:(a + 1) * P], ident[:, :])
                ins.then_inc(side_ready, 1)
                yield

            def mm(dst, a, b, start, stop):
                return pe.matmul(dst, a, b, start=start, stop=stop, skip_group_check=True)

            def sb_work(l):
                for c in range(SB_HEADS // 2):
                    k = 4 * l + c
                    if c == 0:
                        pe.wait_ge(head_done, len(NORMED) * l + 3)
                        pe.wait_ge(taken["act"], nth_of("sb_v", l))

                    def logits(stop):
                        for h in range(2):
                            r = slice(h * SB_DH, (h + 1) * SB_DH)
                            mm(ps[:, h * BW:h * BW + SEQ], kT[r, c, 0:P], qT[r, c, :], True, stop)
                            ins = mm(ps[:, h * BW + SEQ:h * BW + 384], kT[r, c, P:SEQ],
                                     qT[r, c, P:SEQ], False, stop)
                        return ins

                    enter()
                    logits(True).then_inc(side_ready, 1)
                    yield
                    yield
                    enter()
                    logits(False)
                    pe.wait_ge(sb_um, k + 1)
                    for h in range(2):
                        mm(ps[:, h * BW:h * BW + 384], neg_tri[:, :], sb_u[:, h, :], False, False)
                        ins = mm(ps[:, h * BW + P:h * BW + SEQ], neg_one[:, :], sb_u[:, h, SEQ:384],
                                 False, True)
                    ins.then_inc(side_ready, 1)
                    yield
                    yield
                    enter()
                    pe.wait_ge(sb_wm, k + 1)
                    for h in range(2):
                        r = slice(h * SB_DH, (h + 1) * SB_DH)
                        v = slice((2 * c + h) * SB_DH, (2 * c + h + 1) * SB_DH)
                        mm(ps[r, 0:SEQ], sv[:, 0, v], sb_w[:, h, 0:SEQ], True, False)
                        ins = mm(ps[r, P:SEQ], sv[:, 1, v], sb_w[:, h, SEQ:384], False, True)
                    ins.then_inc(side_ready, 1)
                    yield

            def gla_work(l):
                enter()
                pe.wait_ge(taken["act"], nth_of("gla_r", l))
                for t in range(NT):
                    ins = mm(ps[0:GATE_RANK, t * P:(t + 1) * P], ga[:, t, :], ident[:, :], True, True)
                ins.then_inc(side_ready, 1)
                yield
                enter()
                pe.wait_ge(gla_at, l + 1)
                for t in range(NT):
                    dst = ps[:, t * 256:(t + 1) * 256]
                    ins = mm(dst, gaT[:, t * P:(t + 1) * P], a_up[:, l, :], t == 0, True)
                ins.then_inc(side_ready, 1)
                yield
                yield
                enter()
                pe.wait_ge(gla_la, l + 1)
                for b in range(2):
                    for t in range(NT):
                        mm(ps[:, b * SEQ + t * P:b * SEQ + (t + 1) * P], la[:, t, b * P:(b + 1) * P],
                           cum_tri[:, :], b == 0 and t == 0, True)
                for t in range(NT):
                    ins = mm(ps[:, BW + t * 256:BW + (t + 1) * 256], rev_tri[:, :], la[:, t, :],
                             t == 0, True)
                ins.then_inc(side_ready, 1)
                yield
                enter()
                for t in range(NT):
                    for a in range(4):
                        ins = pe.transpose(ps[:, t * BW + a * P:t * BW + (a + 1) * P],
                                           gqk[:, t, a * P:(a + 1) * P], ident[:, :])
                ins.then_inc(side_ready, 1)
                yield
                enter()
                pe.wait_ge(gla_dec, l + 1)
                for b in range(2):
                    for t in range(NT):
                        for h in range(2):
                            r = slice(h * GLA_DK, (h + 1) * GLA_DK)
                            cols = slice(t * P, (t + 1) * P)
                            at = (2 + h) * BW + (b * NT + t) * P
                            mm(ps[:, at:at + P], kiT[r, b, cols], qdT[r, b, cols],
                               b == 0 and t == 0, True)
                for c in range(3):
                    t, r = c // 2, slice((c % 2) * GLA_CHUNK, (c % 2 + 1) * GLA_CHUNK)
                    for b in range(2):
                        for h in range(2):
                            head = 2 * b + h
                            at = (c % 2) * BW + (c // 2) * 256 + b * GLA_DV
                            ins = mm(ps[h * GLA_DK:(h + 1) * GLA_DK, at:at + GLA_DV],
                                     kend[r, t, head * GLA_DK:(head + 1) * GLA_DK],
                                     gv[r, t, head * GLA_DV:(head + 1) * GLA_DV],
                                     c < 2 and b == 0, True)
                ins.then_inc(side_ready, 1)
                yield
                yield
                enter()
                pe.wait_ge(gla_mask, l + 1)
                pe.wait_ge(gla_state, l + 1)
                for b in range(2):
                    for t in range(NT):
                        for h in range(2):
                            head, at = 2 * b + h, h * BW + (b * NT + t) * P
                            mm(ps[:, at:at + P], scT[:, h * 4 + b * NT + t, :],
                               gv[:, t, head * GLA_DV:(head + 1) * GLA_DV], b == 0 and t == 0, False)
                for b in range(2):
                    for c in range(1, 4):
                        for h in range(2):
                            r = slice(h * GLA_DK, (h + 1) * GLA_DK)
                            o = slice((c % 2) * GLA_CHUNK, (c % 2 + 1) * GLA_CHUNK)
                            at = h * BW + (b * NT + c // 2) * P
                            ins = mm(ps[o, at:at + P], qdT[r, b, c * GLA_CHUNK:(c + 1) * GLA_CHUNK],
                                     state[r, c - 1, b, :], False, True)
                ins.then_inc(side_ready, 1)
                yield
                yield
                enter()
                pe.wait_ge(gla_scaled, l + 1)
                for t in range(NT):
                    for a in range(4):
                        ins = pe.transpose(ps[:, t * BW + a * P:t * BW + (a + 1) * P],
                                           go[:, t, a * P:(a + 1) * P], ident[:, :])
                ins.then_inc(side_ready, 1)
                yield

            def ca_work(l):
                enter()
                pe.wait_ge(head_done, len(NORMED) * (l + 1))
                for t in range(NT):
                    for h in range(CA_HEADS):
                        at = (t * CA_HEADS + h) * MEM
                        ins = mm(ps[:, at:at + MEM], cqT[:, h, t * P:(t + 1) * P], ckT[:, h, :],
                                 h % 2 == 0, True)
                ins.then_inc(side_ready, 1)
                yield
                yield
                yield
                yield
                enter()
                pe.wait_ge(ca_scaled, l + 1)
                for m in range(NT):
                    for t in range(NT):
                        for h in range(CA_HEADS):
                            at = m * 2 * BW + h * SEQ + t * P
                            ins = pe.transpose(ps[:, at:at + P],
                                               probs[:, t * CA_HEADS + h, m * P:(m + 1) * P],
                                               ident[:, :])
                ins.then_inc(side_ready, 1)
                yield
                yield
                enter()
                pe.wait_ge(ca_pt, l + 1)
                pe.wait_ge(ca_ptv, l + 1)
                for h in range(CA_HEADS):
                    for m in range(NT):
                        ins = mm(ps[:, h * SEQ:(h + 1) * SEQ], cv[:, m, h * CA_DH:(h + 1) * CA_DH],
                                 pT[:, m, h, :], h % 2 == 0 and m == 0, m == NT - 1)
                ins.then_inc(side_ready, 1)
                yield

            def ff_work(width):
                nonlocal ffs
                ffs += 1
                enter()
                pe.wait_ge(ff_h, ffs)
                for t in range(NT):
                    for a in range(width // P):
                        ins = pe.transpose(ps[:, t * BW + a * P:t * BW + (a + 1) * P],
                                           sq[:, t, a * P:(a + 1) * P], ident[:, :])
                ins.then_inc(side_ready, 1)
                yield

            def side_work(p):
                l = p.layer
                for name in side_names(p):
                    yield name, (head_work() if name == "head" else sb_work(l) if name == "sb"
                                 else gla_work(l) if name == "gla" else ca_work(l) if name == "ca"
                                 else ff_work(p.width))

            in_order(side_work, product, {"start": start, "memory": memory, "x_norm": x_norm,
                                          "x_turn": x_turn, "merged": merged,
                                          "ffn_tokens": ffn_norm})

            enter()
            pe.wait_ge(r_assign, 1)
            mm(ps[:, 0:E], utri[:, :], assign[:, 0, :], True, True)
            mm(ps[:, E:2 * E], ones[:, :], assign[:, 0, :], False, False)
            mm(ps[:, E:2 * E], utri[:, :], assign[:, 1, :], False, True)
            mm(ps[:, 2 * E:3 * E], ones[:, :], assign[:, 0, :], False, False)
            mm(ps[:, 2 * E:3 * E], ones[:, :], assign[:, 1, :], False, True).then_inc(side_ready, 1)

            def gather(n, h):
                pe.wait_ge(sel_ready, n * NT + NT)
                for k in range(KT):
                    for t in range(NT):
                        ins = mm(ps[:, DM + k * P:DM + (k + 1) * P],
                                 th[:, h, t, k * P:(k + 1) * P], sel[:, t, :],
                                 k % 4 == 0 and t == 0, t == NT - 1)
                ins.then_inc(gathered, 1)

            def scatter(n):
                pe.wait_ge(selt_ready, n + 1)
                pe.wait_ge(y_lo, n + 1)
                for t in range(NT):
                    for c in range(2):
                        for h in range(2):
                            dst = (1 - t) * DM + c * BW
                            ins = mm(ps[:, dst:dst + BW], selT[:, t * P:(t + 1) * P],
                                     ysp[:, h, c * BW:(c + 1) * BW], h == 0, h == 1)
                ins.then_inc(scattered, 1)

            pe.wait_ge(r_lo, NT)
            gather(0, 0)
            pe.wait_ge(xg_hi, 1)
            gather(0, 1)
            pe.wait_ge(xg_lo, 1)
            pe.wait_ge(r_table, 1)
            slots = pe.value_load(slot_i[0:1, 0:1], min_val=EXPERTS, max_val=SLOTS)
            with pe.Fori(0, slots) as i:
                at = i * EXP_SLABS
                j = 0

                def block_of(bank):
                    nonlocal j
                    n = SLAB // BW
                    for q in range(GU):
                        s = PRE + j
                        pe.wait_ge(lo_ready, at + (s + 1))
                        for kk in range(n):
                            k = q * n + kk
                            cols = slice(kk * BW, (kk + 1) * BW)
                            ins = passes(pa[:, bank * BW:(bank + 1) * BW], xg[:, 0, k, :],
                                         xg[:, 1, k, :], w_hi[:, s % SPLIT, cols],
                                         w_lo[:, s % SPLIT, cols], k == 0, k == KT - 1)
                        ins.then_inc(slab_used, 1)
                        j += 1

                def down(s):
                    nonlocal j
                    pe.wait_ge(e_lo, i * STEPS + (s + 1))
                    for k in range(HT):
                        q = PRE + j
                        pe.wait_ge(lo_ready, at + (q + 1))
                        for c in range(0, DM, BW):
                            ins = passes(ps[:, c:c + BW], hts[buf[s]][:, 0, k, :],
                                         hts[buf[s]][:, 1, k, :], w_hi[:, q % SPLIT, c:c + BW],
                                         w_lo[:, q % SPLIT, c:c + BW], s == 0 and k == 0,
                                         s == STEPS - 1 and k == HT - 1)
                        ins.then_inc(slab_used, 1)
                        j += 1

                for s in range(STEPS + 1):
                    if s == 0:
                        pe.wait_ge(xg_hi, i + 1)
                        pe.wait_ge(xg_lo, i + 1)
                    if s < STEPS:
                        if s > 0:
                            pe.wait_ge(e_silu, i * STEPS + s)
                        block_of(0)
                    if s == 0:
                        scatter(i)
                        for t in range(NT):
                            ins = pe.transpose(pa[:, 2 * BW + t * P:2 * BW + (t + 1) * P],
                                               sel[:, t, :].bitcast(F32), ident[:, :])
                        ins.then_inc(selt_turned, 1)
                    else:
                        pe.wait_ge(e_h, i * STEPS + s)
                        if s > 1:
                            pe.wait_ge(e_lo, i * STEPS + (s - 1))
                        for a in range(HT):
                            ins = pe.transpose(pa[:, 3 * BW + a * P:3 * BW + (a + 1) * P],
                                               hb[:, a * P:(a + 1) * P], ident[:, :])
                        ins.then_inc(e_turned, 1)
                    if s < STEPS:
                        block_of(1)
                    if s == 1:
                        pe.wait_ge(added, i * NT + NT)
                    if s == STEPS - 1:
                        gather(i + 1, 0)
                    if s > 0:
                        down(s - 1)
                    if s == STEPS - 1:
                        pe.wait_ge(xg_hi, i + 2)
                        gather(i + 1, 1)
            scatter(slots)


_INS = ["x", "mem", "mix_norm_g", "w_in", "sb_q_g", "sb_k_g", "gla_a_up", "gla_a_b", "gla_o_g",
        "ca_q_g", "ca_k_g", "mem_norm_g", "w_mem_kv", "w_br_sb", "w_br_gla", "w_br_ca", "w_out",
        "ffn_norm_g", "ff_w_gate_up", "ff_w_down", "moe_w_router", "moe_w_gate_up", "moe_w_down"]


def kernel(**inputs):
    import numpy as np
    from concourse import bacc
    from concourse.bass_utils import run_bass_kernel_spmd

    nc = bacc.Bacc("TRN2", target_bir_lowering=False, num_devices=1)
    arrays, args = {}, []
    for name in _INS:
        a = np.ascontiguousarray(inputs[name])
        arrays[f"in_{name}"] = a
        args.append(nc.dram_tensor(f"in_{name}", a.shape, mybir.dt.from_np(a.dtype),
                                   kind="ExternalInput").ap())
    out = nc.dram_tensor("out", [1, SEQ, DM], F32, kind="ExternalOutput").ap()
    trunk(nc, *args, out)
    return run_bass_kernel_spmd(nc, [arrays], core_ids=[0]).results[0]["out"]
```

```python
from contextlib import ExitStack

import concourse.bass as bass
from concourse import mybir

F32 = mybir.dt.float32
F32R = mybir.dt.float32r
I32 = mybir.dt.int32
U32 = mybir.dt.uint32
ALU = mybir.AluOpType
ACT = mybir.ActivationFunctionType
AX = mybir.AxisListType

P = 128
SEQ, DM, MEM = 256, 1024, 256
NT = SEQ // P
KT = DM // P
LAYERS = 2
EPS = 1e-6
BW = 512
SB_HEADS, SB_DH = 8, 64
GLA_HEADS, GLA_DK, GLA_DV, GLA_CHUNK, GATE_RANK, GATE_TAU = 4, 64, 128, 64, 16, 16.0
CA_HEADS, CA_DH = 4, 128
BRANCHES = 3
D_FF, EXPERTS, D_EXP = 2816, 8, 3584

C_SBQ, C_SBK, C_SBV, C_GQK, C_GV = 0, BW, 2 * BW, 3 * BW, 4 * BW
C_GA = C_GV + GLA_HEADS * GLA_DV
C_GR = C_GA + GATE_RANK
C_CAQ = C_GR + GLA_HEADS * GLA_DV
C_GATE = C_CAQ + CA_HEADS * CA_DH

SLAB = 1024
RAW, SPLIT = 5, 5
AHEAD = SPLIT - 1
CA_DELAY = 6
GROUP = 4
EXP_RAW, EXP_SPLIT = 21, 4
EXP_AHEAD = EXP_SPLIT - 1

FF_BLOCKS = [(c, min(BW, D_FF - c)) for c in range(0, D_FF, BW)]
FF_PARTS = [FF_BLOCKS[:3], FF_BLOCKS[3:]]
FF_KT = 3 * BW // P

STEPS = D_EXP // BW
HT = BW // P
GU = KT * BW // SLAB
EXP_SLABS = STEPS * (2 * GU + HT)
assert EXP_SLABS % EXP_RAW == 0 and EXP_SLABS % EXP_SPLIT == 0
CAP = P
OVER = 3
SLOTS = EXPERTS + OVER
TURNS = 4
BIAS = 32
GAINS = 16 * LAYERS * 9


class Product:

    def __init__(self, name, layer, kind, lhs, slabs, width, banks, taker):
        self.name, self.layer, self.kind, self.lhs = name, layer, kind, lhs
        self.slabs, self.width, self.banks, self.taker = slabs, width, banks, taker
        n = len(slabs)
        if name.startswith("branch") or name == "out":
            sizes = [min(GROUP, n - i) for i in range(0, n, GROUP)]
        elif name == "ff_down":
            sizes = [GROUP] + [1] * (n - 2 * GROUP) + [GROUP]
        else:
            sizes = [1] * n
        self.set_groups(sizes, {i for i, k in enumerate(sizes) if k > 1})

    def set_groups(self, sizes, by_tile):
        self.groups = [range(sum(sizes[:i]), sum(sizes[:i + 1])) for i in range(len(sizes))]
        self.by_tile = by_tile


def product_table(w_in, w_mem_kv, w_br, w_out, ff_gu, ff_down, w_router):
    table = []

    def add(name, layer, kind, lhs, slabs, width, banks, taker):
        p = Product(name, layer, kind, lhs, slabs, width, banks, taker)
        p.first = sum(len(q.slabs) for q in table)
        p.end = p.first + len(slabs)
        p.before = [q for q in table if q.banks & banks][-3:]
        p.nth = sum(q.taker == taker for q in table) + 1
        table.append(p)

    pairs = [frozenset((0, 1)), frozenset((2, 3))]
    four = frozenset(range(4))
    turn = [0]

    def cols(name, layer, w, c, width, lhs, taker, pair=None):
        if pair is None:
            pair = turn[0] % 2
            turn[0] += 1
        v = w.rearrange("(k p) n -> p k n", p=P)[:, :, c:c + width]
        if width < 256:
            slabs = [v]
        else:
            n = SLAB // width
            slabs = [v[:, k:k + n, :] for k in range(0, KT, n)]
        add(name, layer, "cols", lhs, slabs, width, pairs[pair], taker)

    def rows(name, layer, w, r, n, lhs, banks):
        slabs = [w[r + P * k:r + P * (k + 1), :] for k in range(n)]
        add(name, layer, "rows", lhs, slabs, DM, banks, "rows")

    for l in range(LAYERS):
        cols("mem_k", l, w_mem_kv[l], 0, BW, "xt0", "act")
        cols("mem_v", l, w_mem_kv[l], BW, BW, "xt0", "act")
        for name, c, width in (("sb_q", C_SBQ, BW), ("sb_k", C_SBK, BW), ("sb_v", C_SBV, BW),
                               ("gla_qk", C_GQK, BW), ("ca_q", C_CAQ, BW), ("gla_v", C_GV, BW),
                               ("gla_a", C_GA, GATE_RANK), ("gla_r", C_GR, BW)):
            cols(name, l, w_in[l], c, width, "xt1", "act")
        for b in range(BRANCHES):
            for h in range(2):
                cols(f"gate{h}", l, w_in[l], C_GATE + b * DM + h * BW, BW, "xt1", "act")
            rows(f"branch{b}", l, w_br[b][l], 0, 4, f"ot{b % 2}", four)
        rows("out", l, w_out[l], 0, KT, "xt0", four)
        if l == 0:
            for part in FF_PARTS:
                for c, width in part:
                    cols("ff_gate", l, ff_gu, c, width, "xt0", "act", 0)
                    cols("ff_up", l, ff_gu, D_FF + c, width, "xt0", "dve", 1)
                rows("ff_down", l, ff_down, part[0][0], sum(x[1] for x in part) // P, "ht", four)
        else:
            cols("router", l, w_router, 0, EXPERTS, "xt0", "dve")
    [p for p in table if p.name == "ff_gate"][0].set_groups([GROUP], {0})
    return table


def trunk(nc, x_in, mem_in, mix_norm_g, w_in, sb_q_g, sb_k_g, gla_a_up, gla_a_b, gla_o_g, ca_q_g,
          ca_k_g, mem_norm_g, w_mem_kv, w_br_sb, w_br_gla, w_br_ca, w_out, ffn_norm_g, ff_gate_up,
          ff_down, moe_router, moe_gate_up, moe_down, out):
    table = product_table(w_in, w_mem_kv, (w_br_sb, w_br_gla, w_br_ca), w_out, ff_gate_up[0],
                          ff_down[0], moe_router[0])
    flat = [s for p in table for s in p.slabs]
    PRE = len(flat)
    tokens = x_in[0].rearrange("(t p) d -> p t d", p=P)
    memory_in = mem_in[0].rearrange("(t p) d -> p t d", p=P)
    result = out[0].rearrange("(t p) d -> p t d", p=P)

    with ExitStack() as ctx:
        def sb(name, shape, dt=F32):
            return ctx.enter_context(nc.sbuf_tensor(name, shape, dt))

        def sem(name):
            return ctx.enter_context(nc.semaphore(name))

        w_raw = sb("w_raw", [P, RAW, SLAB])
        w_hi = sb("w_hi", [P, SPLIT, SLAB], F32R)
        w_lo = sb("w_lo", [P, SPLIT, SLAB], F32R)
        xs = sb("xs", [P, NT, DM])
        hn = sb("hn", [P, NT, DM])
        gain = sb("gain", [P, DM])
        gates = sb("gates", [P, NT, DM])
        tok = sb("tok", [P, NT, BW])
        sq = sb("sq", [P, NT, BW])
        qT = sb("qT", [P, 4, SEQ])
        kT = sb("kT", [P, 4, SEQ])
        sv = sb("sv", [P, NT, BW])
        gqk = sb("gqk", [P, NT, BW])
        gv = sb("gv", [P, NT, BW])
        gr = sb("gr", [P, NT, BW])
        cqT = sb("cqT", [P, CA_HEADS, SEQ])
        ckT = sb("ckT", [P, CA_HEADS, MEM])
        cv = sb("cv", [P, NT, BW])
        scr = sb("scr", [P, 5120])
        head_gains = sb("head_gains", [P, LAYERS, 5])
        a_up = sb("a_up", [BIAS + 1, LAYERS, GLA_HEADS * GLA_DK])
        gaT = sb("gaT", [BIAS + 1, SEQ])
        ms = sb("ms", [P, 8])
        rstd = sb("rstd", [P, 8])
        hms, hrs = sb("hms", [P, 16]), sb("hrs", [P, 16])
        half = sb("half", [P, 16])
        nms, nrstd = sb("nms", [P, NT]), sb("nrstd", [P, NT])
        ident = sb("ident", [P, P])
        neg_tri = sb("neg_tri", [P, P])
        neg_one = sb("neg_one", [P, P])
        cum_tri = sb("cum_tri", [P, P])
        rev_tri = sb("rev_tri", [P, P])
        xt0 = sb("xt0", [P, 2, KT, SEQ], F32R)
        r1 = sb("r1", [P, 8192], F32R)
        xt1 = r1[:, 0:4096].rearrange("p (s k t) -> p s k t", s=2, k=KT)
        ot = [r1[:, 4096 + 2048 * i:6144 + 2048 * i].rearrange("p (s k t) -> p s k t", s=2, k=4)
              for i in range(2)]
        ht = r1[:, 0:2 * FF_KT * SEQ].rearrange("p (s k t) -> p s k t", s=2, k=FF_KT)

        def view(a, *dims):
            n = 1
            for d in dims:
                n *= d
            v = scr[:, a:a + n]
            names = "abc"[:len(dims)]
            if len(dims) == 1:
                return v
            return v.rearrange(f"p ({' '.join(names)}) -> p {' '.join(names)}",
                               **{k: d for k, d in zip(names[1:], dims[1:])})

        sb_u, sb_w, sb_e = view(0, 2, 384), view(768, 2, 384), view(1536, 2, 384)
        la, lg = view(0, NT, 256), view(512, NT, 256)
        ecT, einvT = view(1024, 2, SEQ), view(1536, 2, SEQ)
        erev, kend = view(2048, NT, 256), view(2560, NT, 256)
        qdT, kiT = view(3072, 2, SEQ), view(3584, 2, SEQ)
        scT = view(4096, 8, P)
        state = view(1536, 3, 2, GLA_DV)
        go = view(0, NT, BW)
        probs = view(0, 8, MEM)
        pT = view(2048, NT, CA_HEADS, SEQ)
        th = xt0[:, :, :, :].rearrange("p s k t -> p (s k t)").rearrange(
            "p (s t d) -> p s t d", s=2, t=NT)
        xg = r1[:, 0:2048].rearrange("p (s k c) -> p s k c", s=2, k=KT)
        hts = [r1[:, 2048 + 1024 * i:3072 + 1024 * i].rearrange("p (s k c) -> p s k c", s=2, k=HT)
               for i in range(3)]
        ysp = r1[:, 5120:7168].rearrange("p (s d) -> p s d", s=2)
        sel = r1[:, 7168:7424].rearrange("p (t c) -> p t c", t=NT)
        selT = r1[:, 7424:7680]
        buf = [0, 1] * 3 + [2]
        hs, hb = tok[:, 0, :], sq[:, 0, :]
        utri, ones = neg_tri, neg_one
        iota_c = rev_tri
        small = view(0, 512)

        def sm(a, *dims):
            n = 1
            for d in dims:
                n *= d
            v = small[:, a:a + n]
            return v if len(dims) == 1 else v.rearrange("p (a b) -> p a b", b=dims[1])

        E = EXPERTS
        logit, top, pick1, pick2 = (sm(16 * i, NT, E) for i in range(4))
        assign, topi = sm(64, NT, E), sm(80, NT, E)
        iota_e = sm(96, E)
        w1, w2, wd = sm(104, NT), sm(106, NT), sm(108, NT)
        over, oidx, ozero = sm(112, E), sm(120, E), sm(128, E)
        slotf = sm(136, 1 + OVER)
        logitT = gaT[0:E, :]
        order = sm(140, OVER)
        mk, mtmp = sm(144, OVER, E), sm(168, OVER, E)
        slot_pos, slot_comb = sm(192, NT, SLOTS + 1), sm(216, NT, SLOTS + 1)
        slot_i = sb("slot_i", [1, 4], I32)
        topu = sb("topu", [P, NT, E], U32)

        pa = ctx.enter_context(nc.psum_tensor("pa", [P, 4 * BW], F32))
        ps = ctx.enter_context(nc.psum_tensor("ps", [P, 4 * BW], F32))

        raw_ready = [sem(f"raw_ready{i}") for i in range(RAW)]
        hi_ready, lo_ready, slab_used = sem("hi_ready"), sem("lo_ready"), sem("slab_used")
        taken = {"act": sem("act_took"), "dve": sem("dve_took"), "rows": sem("tile_took")}
        tile_done = sem("tile_done")
        side_ready, side_free = sem("side_ready"), sem("side_free")
        first_tile = [sem("mem_tile0_loaded"), sem("mem_tile1_loaded")]
        mem_reloaded = sem("mem_reloaded")
        x_loaded, gain_loaded, gains_loaded = (sem(n) for n in (
            "x_loaded", "gain_loaded", "gains_loaded"))
        consts = sem("consts")
        norm_sq, norm_ms, norm_rs, norm_done = (sem(f"norm_{n}") for n in ("sq", "ms", "rs", "done"))
        turn_ready, turn_hi, turn_lo = sem("turn_ready"), sem("turn_hi"), sem("turn_lo")
        head_ms, head_rs, head_scaled, head_done = (sem(f"head_{n}") for n in (
            "ms", "rs", "scaled", "done"))
        sb_sp, sb_uu, sb_um, sb_min, sb_exp, sb_wm, sb_hi = (sem(f"sb_{n}") for n in (
            "softplus", "u", "u_masked", "arg", "weight", "weight_masked", "hi"))
        gla_lg, gla_la, gla_exp, gla_dec, gla_sc, gla_zero, gla_mask, gla_state, \
            gla_o, gla_scaled, gla_hi = (sem(f"gla_{n}") for n in (
                "lg", "la", "exp", "dec", "scores", "zero", "masked", "states", "o",
                "scaled", "hi"))
        ca_max, ca_exp, ca_scaled, ca_pt, ca_ptv, ca_hi = (sem(f"ca_{n}") for n in (
            "max", "exp", "scaled", "pT_act", "pT_dve", "hi"))
        branch_lo = sem("branch_lo")
        merge_step = sem("merge_step")
        ff_h, ff_hi, ff_lo = (sem(f"ff_{n}") for n in ("h", "hi", "lo"))
        act_step, dve_step, pool_step = sem("act_step"), sem("dve_step"), sem("pool_step")
        r_const, r_hi, r_lo, r_assign, r_wd, r_table = (sem(f"route_{n}") for n in (
            "consts", "tokens_hi", "tokens_lo", "assigned", "weights", "table"))
        sel_ready, gathered, xg_hi, xg_lo, selt_turned, selt_ready = (sem(n) for n in (
            "sel_ready", "gathered", "xg_hi", "xg_lo", "selt_turned", "selt_ready"))
        y_cleared = sem("y_cleared")
        e_silu, e_h, e_turned, e_hi, e_lo, y_hi, y_lo, scattered, added = (sem(n) for n in (
            "e_silu", "e_h", "e_turned", "e_hi", "e_lo", "y_hi", "y_lo", "scattered", "added"))
        stored = sem("stored")

        more_ready = [sem(f"more_ready{i}") for i in range(EXP_RAW)]

        def raw_slot(j):
            return w_raw[:, j % RAW, :]

        exp_hi, exp_lo = ([w[:, (PRE + n) % SPLIT, :] for n in range(EXP_SPLIT)]
                          for w in (w_hi, w_lo))
        def fresh(slots):
            n = len(exp_slots)
            return [(v, more_ready[n + k], 0) for k, v in enumerate(slots)]

        exp_slots = []
        exp_slots += fresh([b[:, :, :].rearrange("p a b -> p (a b)")
                            for b in (qT, kT, sv, gqk, gv, gr, cqT, ckT, cv)])
        exp_slots += fresh([scr[:, SLAB * n:SLAB * (n + 1)] for n in range(1, 5)])
        W_RAW_SLOT = len(exp_slots)
        exp_slots += [(raw_slot(PRE + n), raw_ready[(PRE + n) % RAW],
                       16 * len(range((PRE + n) % RAW, PRE, RAW))) for n in range(RAW)]
        GATES_SLOT = len(exp_slots)
        exp_slots += fresh([gates[:, 0, :], gates[:, 1, :], gain[:, :]])
        assert len(exp_slots) == EXP_RAW

        sizes = []
        for p in table:
            for s in p.slabs:
                sizes.append(KT * p.width if p.width < 256 else SLAB)

        block = ctx.enter_context(nc.Block())

        def in_order(side_work, product, alone):
            waiting = []

            def side():
                while waiting:
                    try:
                        next(waiting[0][1])
                        return
                    except StopIteration:
                        waiting.pop(0)

            def finish(name=None):
                while waiting and (name is None or any(n == name for n, _ in waiting)):
                    side()

            alone["start"]()
            for p in table:
                if p.name == "mem_k":
                    finish()
                    alone["x_norm"](p.layer)
                elif p.name == "mem_v":
                    waiting.insert(0, ("x_turn", alone["x_turn"](p.layer)))
                elif p.name == "sb_q":
                    finish("x_turn")
                elif p.name in ("branch0", "branch1", "branch2"):
                    finish({"branch0": "sb", "branch1": "gla", "branch2": "ca"}[p.name])
                elif after_norm(p):
                    finish()
                    alone["ffn_tokens"](p.layer)
                elif p is last_down:
                    waiting.append(("memory", alone["memory"](p.layer + 1)))
                product(p, side, finish)
                for name, work in side_work(p):
                    waiting.insert(0 if name == "head" else len(waiting), (name, work))
            finish()

        first_gate = [p for p in table if p.name == "ff_gate"][0]
        last_down = [p for p in table if p.name == "ff_down"][-1]

        def side_names(p):
            return {"mem_k": ["head"], "sb_q": ["head"], "sb_k": ["head"], "ca_q": ["head"],
                    "sb_v": ["sb"], "gla_r": ["gla", "ca"], "ff_up": ["ff"]}.get(p.name, [])

        NORMED = ("mem_k", "sb_q", "sb_k", "ca_q")

        def split_slabs(p, splits_until, side, take, edge):
            for g, group in enumerate(p.groups):
                s = p.first + group[0] + 1 + AHEAD
                splits_until(s)
                if g not in p.by_tile:
                    side()
                    continue
                if g == 0:
                    edge("first")
                side()
                side()
                final = g == len(p.groups) - 1
                if p.kind == "rows" and final:
                    take(0)
                    edge("tile0")
                splits_until(s + 1)
                splits_until(s + 2)
                side()
                if final:
                    edge("tile1")
                splits_until(s + 3)
                side()
            if p.kind == "rows":
                take(1)

        def pause(n):
            for _ in range(n):
                yield

        def after_norm(p):
            return p is first_gate or p.name == "router"

        def nth_of(name, l):
            return [p.nth for p in table if p.name == name and p.layer == l][0]

        def acts_before(p):
            return sum(q.taker == "act" for q in table[:table.index(p)])

        def residual(name, l, t):
            q = [q for q in table if q.name == name and q.layer == l][-1]
            return NT * (q.nth - 1) + t + 1

        def head_number(p):
            return [q for q in table if q.name in NORMED].index(p) + 1

        def head_dim(p):
            return SB_DH if p.name in ("sb_q", "sb_k") else CA_DH

        def hidden_before(p):
            return sum(len(FF_PARTS[i]) for i in range([q for q in table if q.name == "ff_down"]
                                                       .index(p)))

        def hidden_tile(p):
            c = [q for q in table if q.name == "ff_up"].index(p)
            part = [x for x in FF_PARTS if FF_BLOCKS[c] in x][0]
            return (FF_BLOCKS[c][0] - part[0][0]) // P

        @block.sync
        def _(sp):
            for t in range(NT):
                sp.dma_start(hn[:, t, :], memory_in[:, t, :]).then_inc(first_tile[t], 16)
            for s, src in enumerate(flat):
                if s == 2:
                    sp.dma_start(xs[:, :, :], tokens).then_inc(x_loaded, 16)
                if s >= RAW:
                    sp.wait_ge(lo_ready, s - RAW + 1)
                dst = raw_slot(s)[:, 0:sizes[s]]
                if len(src.shape) == 3:
                    dst = dst.rearrange("p (k n) -> p k n", k=src.shape[1])
                sp.dma_start(dst, src).then_inc(raw_ready[s % RAW], 16)

            def expert_slabs(e, i):
                gate_up = moe_gate_up[0].rearrange("e (k p) n -> e p k n", p=P)
                j = 0

                def load(src, k):
                    nonlocal j
                    dst, ready, _ = exp_slots[j % EXP_RAW]
                    sp.wait_ge(lo_ready, i * EXP_SLABS + (PRE + j - EXP_RAW + 1))
                    if j == W_RAW_SLOT:
                        sp.wait_ge(lo_ready, PRE)
                    if j == GATES_SLOT:
                        sp.wait_ge(norm_done, NT * (3 * LAYERS))
                    if k > 1:
                        dst = dst.rearrange("p (k n) -> p k n", k=k)
                    sp.dma_start(dst, src).then_inc(ready, 16)
                    j += 1

                def cols(c):
                    n = SLAB // BW
                    for k in range(0, KT, n):
                        load(gate_up[bass.ds(e, 1), :, k:k + n, c:c + BW]
                             .rearrange("e p k n -> p (e k) n"), n)

                def rows(s):
                    for k in range(HT * s, HT * (s + 1)):
                        load(moe_down[0][bass.ds(e, 1), P * k:P * (k + 1), :]
                             .rearrange("e p n -> p (e n)"), 1)

                for s in range(STEPS):
                    cols(BW * s)
                    cols(D_EXP + BW * s)
                    if s > 0:
                        rows(s - 1)
                rows(STEPS - 1)

            sp.wait_ge(merge_step, NT * BRANCHES * LAYERS)
            with sp.Fori(0, EXPERTS) as e:
                expert_slabs(e, e)
            sp.wait_ge(r_table, 1)
            slots = sp.value_load(slot_i[0:1, 0:1], min_val=EXPERTS, max_val=SLOTS)
            with sp.If(slots > EXPERTS) as _:
                with sp.Fori(EXPERTS, slots) as i:
                    e = sp.value_load(slot_i[0:1, bass.ds(i - (EXPERTS - 1), 1)], min_val=0,
                                      max_val=EXPERTS - 1)
                    expert_slabs(e, i)
            for t in range(NT):
                sp.wait_ge(added, slots * NT + (t + 1))
                sp.dma_start(result[:, t, :], xs[:, t, :]).then_inc(stored, 16)
            sp.wait_ge(stored, NT * 16)

        @block.gpsimd
        def _(pool):
            steps = 0

            def link(ins):
                nonlocal steps
                steps += 1
                ins.then_inc(pool_step, 1)
                pool.wait_ge(pool_step, steps)

            gain_order = [g[l] for l in range(LAYERS) for g in (mem_norm_g, mix_norm_g, ffn_norm_g)]

            def load_gain(k):
                if k > 0:
                    pool.wait_ge(norm_done, NT * k)
                pool.dma_start(gain[:, :], gain_order[k].rearrange("(o d) -> o d", o=1)
                               .broadcast_to([P, DM])).then_inc(gain_loaded, 16)

            def start():
                load_gain(0)
                link(pool.memset(half[:, :], -0.5))
                link(pool.memset(ident[:, :], 0.0))
                pool.affine_select(out=ident[:, :], in_=ident[:, :], compare_op=ALU.not_equal,
                                   fill=1.0, base=0, pattern=[[-1, P]], channel_multiplier=1)\
                    .then_inc(consts, 1)
                pool.wait_ge(consts, 1)
                inverse_root()
                load_gain(1)

            def mixer_constants():
                link(pool.memset(a_up[:, :, :], 0.0))
                for l in range(LAYERS):
                    for i, (g, n) in enumerate(((sb_q_g, SB_DH), (sb_k_g, SB_DH), (gla_o_g, GLA_DV),
                                                (ca_q_g, CA_DH), (ca_k_g, CA_DH))):
                        for r in range(0, P, n):
                            pool.dma_start(head_gains[r:r + n, l, i:i + 1],
                                           g[l].rearrange("(d o) -> d o", o=1),
                                           allow_slow_non_contiguous=True).then_inc(gains_loaded, 16)
                    pool.dma_start(a_up[0:GATE_RANK, l, :], gla_a_up[l]).then_inc(gains_loaded, 16)
                    pool.dma_start(a_up[BIAS:BIAS + 1, l, :], gla_a_b[l]
                                   .rearrange("(o d) -> o d", o=1)).then_inc(gains_loaded, 16)
                link(pool.memset(gaT[:, :], 0.0))
                link(pool.memset(gaT[BIAS:BIAS + 1, :], 1.0))
                link(pool.memset(neg_tri[:, :], -1.0))
                link(pool.memset(neg_one[:, :], -1.0))
                link(pool.memset(cum_tri[:, :], 1.0 / GATE_TAU))
                link(pool.memset(rev_tri[:, :], 1.0 / GATE_TAU))
                link(pool.affine_select(out=neg_tri[:, :], in_=neg_tri[:, :], compare_op=ALU.is_ge,
                                        fill=0.0, base=0, pattern=[[-1, P]], channel_multiplier=1))
                link(pool.affine_select(out=cum_tri[:, :], in_=cum_tri[:, :], compare_op=ALU.is_ge,
                                        fill=0.0, base=0, pattern=[[1, P]], channel_multiplier=-1))
                link(pool.affine_select(out=rev_tri[:, :], in_=rev_tri[:, :], compare_op=ALU.is_gt,
                                        fill=0.0, base=0, pattern=[[-1, P]], channel_multiplier=1))
                link(pool.memset(cum_tri[0:GLA_CHUNK, GLA_CHUNK:P], 0.0))
                pool.memset(rev_tri[GLA_CHUNK:P, 0:GLA_CHUNK], 0.0).then_inc(consts, 1)
                pool.wait_ge(consts, 2)

            norms = 0

            def inverse_root():
                nonlocal norms
                for t in range(NT):
                    norms += 1
                    pool.wait_ge(norm_ms, norms)
                    pool.tensor_tensor(nrstd[:, t:t + 1], nms[:, t:t + 1], half[:, 0:1], ALU.pow)\
                        .then_inc(norm_rs, 1)
                    pool.wait_ge(norm_rs, norms)

            def memory(l):
                inverse_root()
                load_gain(3 * l + 1)
                yield
                yield

            def x_norm(l):
                inverse_root()
                if l == 0:
                    mixer_constants()
                load_gain(3 * l + 2)

            def x_turn(l):
                yield
                yield

            def ffn_norm(l):
                inverse_root()
                if l + 1 < LAYERS:
                    load_gain(3 * l + 3)
                    pool.wait_ge(turn_ready, NT * TURNS * (l + 1))
                    pool.dma_start(hn[:, :, :], memory_in).then_inc(mem_reloaded, 16)

            def product(p, side, finish):
                for _ in p.slabs:
                    side()
                if p.name in NORMED:
                    finish("head")
                    head_norm(NT * BW // head_dim(p), hrs, hms)

            heads = 0

            def head_norm(n, dst, src):
                nonlocal heads
                heads += 1
                pool.wait_ge(head_ms, heads)
                pool.tensor_tensor(dst[:, 0:n], src[:, 0:n], half[:, 0:n], ALU.pow)\
                    .then_inc(head_rs, 1)
                pool.wait_ge(head_rs, heads)

            def head_work():
                yield
                yield
                yield

            def sb_work(l):
                for c in range(SB_HEADS // 2):
                    k = 4 * l + c
                    pool.wait_ge(sb_uu, k + 1)
                    link(pool.affine_select(out=sb_u[:, :, 0:P], in_=sb_u[:, :, 0:P],
                                            compare_op=ALU.is_gt, fill=0.0, base=0,
                                            pattern=[[0, 2], [1, P]], channel_multiplier=-1))
                    pool.affine_select(out=sb_u[:, :, SEQ:SEQ + P], in_=sb_u[:, :, SEQ:SEQ + P],
                                       compare_op=ALU.is_gt, fill=0.0, base=0,
                                       pattern=[[0, 2], [1, P]], channel_multiplier=-1)\
                        .then_inc(sb_um, 1)
                    pool.wait_ge(sb_um, k + 1)
                    yield
                    yield
                    pool.wait_ge(sb_exp, k + 1)
                    link(pool.affine_select(out=sb_w[:, :, 0:P], in_=sb_w[:, :, 0:P],
                                            compare_op=ALU.is_gt, fill=0.0, base=0,
                                            pattern=[[0, 2], [1, P]], channel_multiplier=-1))
                    pool.affine_select(out=sb_w[:, :, SEQ:SEQ + P], in_=sb_w[:, :, SEQ:SEQ + P],
                                       compare_op=ALU.is_gt, fill=0.0, base=0,
                                       pattern=[[0, 2], [1, P]], channel_multiplier=-1)\
                        .then_inc(sb_wm, 1)
                    pool.wait_ge(sb_wm, k + 1)
                    yield
                    yield
                    yield

            def gla_work(l):
                yield
                yield
                yield
                pool.wait_ge(gla_la, l + 1)
                pool.memset(scT, 0.0).then_inc(gla_zero, 1)
                pool.wait_ge(gla_zero, l + 1)
                yield
                yield
                pool.wait_ge(gla_sc, l + 1)
                pool.affine_select(out=scT, in_=scT, compare_op=ALU.is_ge, fill=0.0, base=0,
                                   pattern=[[0, 8], [1, P]], channel_multiplier=-1)\
                    .then_inc(gla_mask, 1)
                pool.wait_ge(gla_mask, l + 1)
                yield
                yield
                head_norm(NT * GLA_HEADS, rstd, ms)
                yield
                yield
                yield
                yield

            def ca_work(l):
                for _ in range(CA_DELAY + 7):
                    yield

            def ff_work():
                yield

            def side_work(p):
                l = p.layer
                for name in side_names(p):
                    yield name, (head_work() if name == "head" else sb_work(l) if name == "sb"
                                 else gla_work(l) if name == "gla" else ca_work(l) if name == "ca"
                                 else ff_work())

            in_order(side_work, product, {"start": start, "memory": memory, "x_norm": x_norm,
                                          "x_turn": x_turn, "ffn_tokens": ffn_norm})

            pool.wait_ge(turn_ready, NT * TURNS * LAYERS)
            link(pool.memset(ones[:, :], 1.0))
            link(pool.memset(utri[:, :], 1.0))
            link(pool.affine_select(out=utri[:, :], in_=utri[:, :], compare_op=ALU.is_gt, fill=0.0,
                                    base=0, pattern=[[1, P]], channel_multiplier=-1))
            link(pool.iota(iota_c[:, :], pattern=[[1, P]], base=0, channel_multiplier=0,
                           allow_small_or_imprecise_dtypes=True))
            link(pool.iota(order, pattern=[[1, OVER]], base=1, channel_multiplier=0,
                           allow_small_or_imprecise_dtypes=True))
            pool.iota(iota_e, pattern=[[1, E]], base=0, channel_multiplier=0,
                      allow_small_or_imprecise_dtypes=True).then_inc(r_const, 1)

        @block.scalar
        def _(act):
            steps = 0

            def link(ins):
                nonlocal steps
                steps += 1
                ins.then_inc(act_step, 1)
                act.wait_ge(act_step, steps)

            def split(s):
                act.wait_ge(raw_ready[s % RAW], 16 * (s // RAW + 1))
                if s >= SPLIT:
                    act.wait_ge(slab_used, s - SPLIT + 1)
                n = sizes[s]
                act.activation(w_hi[:, s % SPLIT, 0:n], raw_slot(s)[:, 0:n], ACT.Copy)\
                    .then_inc(hi_ready, 1)

            done = 0

            def splits_until(n):
                nonlocal done
                while done < min(n, PRE):
                    split(done)
                    done += 1

            visits = 0

            def visit():
                nonlocal visits
                visits += 1
                act.wait_ge(side_ready, visits)
                return visits

            def square(src, t):
                act.activation(gates[:, t, :], src[:, t, :], ACT.Square, accum_out=nms[:, t:t + 1])\
                    .then_inc(norm_sq, 1)

            turns = 0

            def turned(dst, banks, t):
                nonlocal turns
                turns += 1
                act.wait_ge(turn_ready, turns)
                act.activation(dst[:, 0, :, t * P:(t + 1) * P],
                               banks[:, t * DM:(t + 1) * DM].rearrange("p (k t) -> p k t", k=KT),
                               ACT.Copy).then_inc(turn_hi, 1)

            def start():
                for t in range(NT):
                    act.wait_ge(first_tile[t], 16)
                    square(hn, t)
                splits_until(2)
                for t in range(NT):
                    turned(xt0, ps, t)

            def memory(l):
                act.wait_ge(mem_reloaded, 16)
                for t in range(NT):
                    square(hn, t)
                yield
                for t in range(NT):
                    turned(xt0, ps, t)
                yield

            def x_norm(l):
                if l == 0:
                    act.wait_ge(x_loaded, 16)
                for t in range(NT):
                    if l > 0:
                        act.wait_ge(taken["rows"], residual("ff_down", l - 1, t))
                    square(xs, t)

            def x_turn(l):
                yield
                for t in range(NT):
                    turned(xt1, ps, t)
                yield

            def ffn_norm(l):
                last = l == LAYERS - 1
                if not last:
                    turned(xt0, ps, 0)
                act.wait_ge(taken["rows"], residual("out", l, 1))
                square(xs, 1)
                if last:
                    for t in range(NT):
                        turned(xt0, ps, t)

            def edge(p, at):
                if (p.name, at) == ("branch2", "tile1"):
                    turned(xt0, ps, 0)
                elif (p.name, at) == ("out", "first") or (p is first_gate and at == "first"):
                    turned(xt0, ps, 1)
                elif (p.name, at) == ("out", "tile0"):
                    act.wait_ge(taken["rows"], residual("out", p.layer, 0))
                    square(xs, 0)

            def bank(p, t):
                b = min(p.banks)
                return pa[:, (b + t) * BW:(b + t) * BW + p.width]

            gate_use = 0
            table_set = None

            def product(p, side, finish):
                nonlocal gate_use, table_set
                split_slabs(p, splits_until, side, lambda t: None, lambda at: edge(p, at))
                if p.name in NORMED:
                    finish("head")
                if p.taker != "act":
                    return
                act.wait_ge(slab_used, p.end)
                l = p.layer
                if p.name in NORMED:
                    for t in range(NT):
                        act.activation(tok[:, t, :], bank(p, t), ACT.Copy)
                        ins = act.activation(sq[:, t, :], bank(p, t), ACT.Square)
                    ins.then_inc(taken["act"], 1)
                    return
                if p.name == "gla_a":
                    at = min(p.banks) * BW
                    act.activation(gaT[0:GATE_RANK, :], pa[0:GATE_RANK, at:at + SEQ], ACT.Copy)\
                        .then_inc(taken["act"], 1)
                    return
                dst, func = {"mem_v": (cv, ACT.Copy), "sb_v": (sv, ACT.Copy),
                             "gla_qk": (gqk, ACT.Copy), "gla_v": (gv, ACT.Copy),
                             "gla_r": (gr, ACT.Silu),
                             "gate0": (gates[:, :, 0:BW], ACT.Sigmoid),
                             "gate1": (gates[:, :, BW:DM], ACT.Sigmoid),
                             "ff_gate": (tok, ACT.Silu)}[p.name]
                if p.name == "gate0":
                    if gate_use % BRANCHES > 0:
                        act.wait_ge(merge_step, NT * gate_use)
                    gate_use += 1
                if p.name == "ff_gate" and blocks > 0:
                    act.wait_ge(ff_h, blocks)
                if func != ACT.Copy:
                    table_set = func
                for t in range(NT):
                    ins = act.activation(dst[:, t, 0:p.width], bank(p, t), func)
                ins.then_inc(taken["act"], 1)

            def head_work():
                yield
                yield
                visit()
                yield

            def exp_ln_table():
                nonlocal table_set
                if table_set != "natural_log_exp_and_others":
                    table_set = "natural_log_exp_and_others"
                    act.preload_act_table_set(table_set)

            def sb_work(l):
                for c in range(SB_HEADS // 2):
                    k = 4 * l + c
                    exp_ln_table()
                    visit()
                    z = ps[:, 0:2 * BW].rearrange("p (h n) -> p h n", h=2)[:, :, 0:384]
                    link(act.activation(sb_e, z, ACT.Abs))
                    link(act.activation(sb_e, sb_e, ACT.Exp, scale=-1.0))
                    act.activation(sb_e, sb_e, ACT.Ln, bias=1.0).then_inc(sb_sp, 1)
                    yield
                    yield
                    exp_ln_table()
                    visit()
                    act.wait_ge(sb_min, k + 1)
                    act.activation(sb_w, sb_w, ACT.Exp).then_inc(sb_exp, 1)
                    yield
                    yield
                    visit()
                    act.activation(ot[0][:, 0, c, :], ps[:, 0:SEQ], ACT.Copy).then_inc(sb_hi, 1)
                    yield

            def gla_work(l):
                exp_ln_table()
                visit()
                link(act.activation(lg.rearrange("p a b -> p (a b)"), ps[:, 0:BW], ACT.Abs))
                link(act.activation(lg, lg, ACT.Exp, scale=-1.0))
                act.activation(lg, lg, ACT.Ln, bias=1.0).then_inc(gla_lg, 1)
                yield
                yield
                exp_ln_table()
                visit()
                act.activation(ecT.rearrange("p a b -> p (a b)"), ps[:, 0:BW], ACT.Exp)
                act.activation(einvT.rearrange("p a b -> p (a b)"), ps[:, 0:BW], ACT.Exp, scale=-1.0)
                act.activation(erev.rearrange("p a b -> p (a b)"), ps[:, BW:2 * BW], ACT.Exp)\
                    .then_inc(gla_exp, 1)
                yield
                visit()
                yield
                yield
                visit()
                act.wait_ge(gla_zero, l + 1)
                for r in (0, GLA_CHUNK):
                    ins = act.activation(
                        scT[r:r + GLA_CHUNK, :, r:r + GLA_CHUNK],
                        ps[r:r + GLA_CHUNK, 2 * BW:4 * BW].rearrange("p (a i) -> p a i", a=8)
                        [:, :, r:r + GLA_CHUNK], ACT.Copy)
                ins.then_inc(gla_sc, 1)
                yield
                yield
                visit()
                for par in range(2):
                    src = ps[:, par * BW:(par + 1) * BW].rearrange("p (b t d) -> p t b d", b=2, t=NT)
                    for dst, func in ((go, ACT.Copy), (sq[:, :, :], ACT.Square)):
                        d = dst.rearrange("p t (b h d) -> p t b h d", b=2, h=2)[:, :, :, par, :]
                        ins = act.activation(d, src, func)
                ins.then_inc(gla_o, 1)
                yield
                yield
                yield
                visit()
                for t in range(NT):
                    act.activation(ot[1][:, 0, :, t * P:(t + 1) * P],
                                   ps[:, t * BW:(t + 1) * BW].rearrange("p (h t) -> p h t", h=4),
                                   ACT.Copy, scale=head_gains[:, l, 2:3]).then_inc(gla_hi, 1)
                yield

            def ca_work(l):
                yield from pause(CA_DELAY)
                exp_ln_table()
                visit()
                act.wait_ge(ca_max, l + 1)
                for a in range(NT * CA_HEADS):
                    if a == CA_HEADS:
                        yield
                    ins = act.activation(probs[:, a, :], ps[:, a * MEM:(a + 1) * MEM], ACT.Exp,
                                         bias=ms[:, a:a + 1], scale=CA_DH ** -0.5,
                                         accum_out=rstd[:, a:a + 1])
                ins.then_inc(ca_exp, 1)
                yield
                yield
                yield
                visit()
                act.activation(pT[:, 0, :, :].rearrange("p h t -> p (h t)"), ps[:, 0:2 * BW],
                               ACT.Copy).then_inc(ca_pt, 1)
                yield
                yield
                visit()
                act.activation(ot[0][:, 0, :, :].rearrange("p h t -> p (h t)"), ps[:, 0:2 * BW],
                               ACT.Copy).then_inc(ca_hi, 1)
                yield

            blocks = 0

            def ff_work(width, k0):
                nonlocal blocks
                blocks += 1
                visit()
                n = width // P
                for t in range(NT):
                    act.activation(ht[:, 0, k0:k0 + n, t * P:(t + 1) * P],
                                   ps[:, t * BW:t * BW + width].rearrange("p (k t) -> p k t", k=n),
                                   ACT.Copy).then_inc(ff_hi, 1)
                yield

            def side_work(p):
                l = p.layer
                for name in side_names(p):
                    yield name, (head_work() if name == "head" else sb_work(l) if name == "sb"
                                 else gla_work(l) if name == "gla" else ca_work(l) if name == "ca"
                                 else ff_work(p.width, hidden_tile(p)))

            in_order(side_work, product, {"start": start, "memory": memory, "x_norm": x_norm,
                                          "x_turn": x_turn, "ffn_tokens": ffn_norm})

            act.preload_act_table_set("exp_and_others")
            act.wait_ge(slab_used, PRE)
            for t in range(NT):
                act.activation(th[:, 0, t, :], hn[:, t, :], ACT.Copy).then_inc(r_hi, 1)
            act.wait_ge(r_assign, 1)
            act.activation(wd, wd, ACT.Exp).then_inc(r_wd, 1)
            act.preload_act_table_set("silu_and_others")
            act.wait_ge(gathered, 1)
            act.activation(xg[:, 0, :, :].rearrange("p k c -> p (k c)"), ps[:, DM:2 * DM], ACT.Copy)\
                .then_inc(xg_hi, 1)

            act.wait_ge(r_table, 1)
            slots = act.value_load(slot_i[0:1, 0:1], min_val=EXPERTS, max_val=SLOTS)
            with act.Fori(0, slots) as i:
                at = i * EXP_SLABS
                j = 0

                def expert_split(n):
                    nonlocal j
                    while j < min(n, EXP_SLABS):
                        s = PRE + j
                        src, ready, before = exp_slots[j % EXP_RAW]
                        act.wait_ge(ready, i * (16 * EXP_SLABS // EXP_RAW)
                                    + (before + 16 * (j // EXP_RAW + 1)))
                        act.wait_ge(slab_used, at + (s - EXP_SPLIT + 1))
                        act.activation(exp_hi[j % EXP_SPLIT], src, ACT.Copy)\
                            .then_inc(hi_ready, 1)
                        j += 1

                expert_split(EXP_AHEAD)
                act.wait_ge(slab_used, at + PRE)
                act.wait_ge(y_cleared, 1)
                act.activation(ysp[:, 0, :], ps[:, 0:DM], ACT.Copy).then_inc(y_hi, 1)
                used = 0
                for s in range(STEPS + 1):
                    if s < STEPS:
                        for _ in range(GU):
                            used += 1
                            expert_split(used + EXP_AHEAD)
                        act.wait_ge(slab_used, at + (PRE + used))
                        if s > 0:
                            act.wait_ge(e_h, i * STEPS + s)
                        act.activation(hs, pa[:, 0:BW], ACT.Silu).then_inc(e_silu, 1)
                    if s == 0:
                        act.wait_ge(selt_turned, i + 1)
                        act.activation(selT, pa[:, 2 * BW:2 * BW + SEQ], ACT.Copy)\
                            .then_inc(selt_ready, 1)
                    else:
                        act.wait_ge(e_turned, i * STEPS + s)
                        act.activation(hts[buf[s - 1]][:, 0, :, :].rearrange("p k c -> p (k c)"),
                                       pa[:, 3 * BW:4 * BW], ACT.Copy).then_inc(e_hi, 1)
                    if s < STEPS:
                        for _ in range(GU):
                            used += 1
                            expert_split(used + EXP_AHEAD)
                    if s == STEPS - 1:
                        act.wait_ge(gathered, i * 2 + 3)
                        act.wait_ge(slab_used, at + (PRE + used))
                        act.activation(xg[:, 0, :, :].rearrange("p k c -> p (k c)"),
                                       ps[:, DM:2 * DM], ACT.Copy).then_inc(xg_hi, 1)
                    if s > 0:
                        for _ in range(HT):
                            used += 1
                            expert_split(used + EXP_AHEAD)
            act.wait_ge(slab_used, slots * EXP_SLABS + PRE)
            for c in range(0, DM, BW):
                act.activation(ysp[:, 0, c:c + BW], ps[:, c:c + BW], ACT.Copy).then_inc(y_hi, 1)

        @block.vector
        def _(dve):
            steps = 0

            def link(ins):
                nonlocal steps
                steps += 1
                ins.then_inc(dve_step, 1)
                dve.wait_ge(dve_step, steps)

            done = 0

            def splits_until(n):
                nonlocal done
                while done < min(n, PRE):
                    s, w = done, sizes[done]
                    dve.wait_ge(hi_ready, s + 1)
                    dve.tensor_tensor(w_lo[:, s % SPLIT, 0:w], raw_slot(s)[:, 0:w],
                                      w_hi[:, s % SPLIT, 0:w].bitcast(F32), ALU.subtract)\
                        .then_inc(lo_ready, 1)
                    done += 1

            visits = 0

            def visit():
                nonlocal visits
                visits += 1
                dve.wait_ge(side_ready, visits)

            norms = 0

            def mean_square(t):
                dve.wait_ge(norm_sq, norms + t + 1)
                dve.tensor_scalar(nms[:, t:t + 1], nms[:, t:t + 1], 1.0 / DM, EPS, ALU.mult,
                                  ALU.add).then_inc(norm_ms, 1)

            def normalise(src, t):
                nonlocal norms
                dve.wait_ge(norm_rs, norms + t + 1)
                dve.wait_ge(gain_loaded, 16 * (norms // NT + 1))
                dve.scalar_tensor_tensor(out=hn[:, t, :], in0=src[:, t, :], scalar=nrstd[:, t:t + 1],
                                         in1=gain[:, :], op0=ALU.mult, op1=ALU.mult)\
                    .then_inc(norm_done, 1)
                if t == NT - 1:
                    norms += NT

            turns = 0

            def turned(dst, banks, t):
                nonlocal turns
                turns += 1
                dve.wait_ge(turn_hi, turns)
                dve.tensor_tensor(
                    dst[:, 1, :, t * P:(t + 1) * P],
                    banks[:, t * DM:(t + 1) * DM].rearrange("p (k t) -> p k t", k=KT),
                    dst[:, 0, :, t * P:(t + 1) * P].bitcast(F32), ALU.subtract)\
                    .then_inc(turn_lo, 1)
                if banks is ps and t == NT - 1:
                    dve.wait_ge(turn_lo, turns)
                    dve.sem_inc(side_free, 1)

            def start():
                for t in range(NT):
                    dve.wait_ge(first_tile[t], 16)
                    mean_square(t)
                    normalise(hn, t)
                splits_until(2)
                for t in range(NT):
                    turned(xt0, ps, t)

            def memory(l):
                dve.wait_ge(mem_reloaded, 16)
                for t in range(NT):
                    mean_square(t)
                for t in range(NT):
                    normalise(hn, t)
                yield
                for t in range(NT):
                    turned(xt0, ps, t)
                yield

            def x_norm(l):
                if l == 0:
                    dve.wait_ge(x_loaded, 16)
                for t in range(NT):
                    mean_square(t)
                dve.wait_ge(turn_ready, turns)
                for t in range(NT):
                    normalise(xs, t)

            def x_turn(l):
                yield
                for t in range(NT):
                    turned(xt1, ps, t)
                yield

            def ffn_norm(l):
                last = l == LAYERS - 1
                if not last:
                    turned(xt0, ps, 0)
                mean_square(1)
                normalise(xs, 1)
                if last:
                    for t in range(NT):
                        turned(xt0, ps, t)

            def edge(p, at):
                if (p.name, at) == ("branch2", "tile1"):
                    turned(xt0, ps, 0)
                elif (p.name, at) == ("out", "first") or (p is first_gate and at == "first"):
                    turned(xt0, ps, 1)
                elif (p.name, at) == ("out", "tile0"):
                    mean_square(0)
                    normalise(xs, 0)

            tiles_done = 0

            def take(p, t):
                nonlocal tiles_done
                if t == 0:
                    tiles_done += 1
                    dve.wait_ge(tile_done, tiles_done)
                else:
                    dve.wait_ge(slab_used, p.end)
                count = NT * (p.nth - 1) + t + 1
                if p.name in ("out", "ff_down"):
                    dve.tensor_tensor(xs[:, t, :], pa[:, t * DM:(t + 1) * DM], xs[:, t, :], ALU.add)\
                        .then_inc(taken["rows"], 1)
                    dve.wait_ge(taken["rows"], count)
                    return
                b = int(p.name[-1])
                dve.wait_ge(taken["act"], acts_before(p))
                dst = hn if b == 0 else gates
                dve.tensor_tensor(dst[:, t, :], pa[:, t * DM:(t + 1) * DM], gates[:, t, :], ALU.mult)\
                    .then_inc(taken["rows"], 1)
                dve.wait_ge(taken["rows"], count)
                if b == 0:
                    dve.sem_inc(merge_step, 1)
                else:
                    dve.tensor_tensor(hn[:, t, :], hn[:, t, :], gates[:, t, :], ALU.add)\
                        .then_inc(merge_step, 1)
                    dve.wait_ge(merge_step, NT * (BRANCHES * p.layer + b) + t + 1)

            def product(p, side, finish):
                split_slabs(p, splits_until, side, lambda t: take(p, t), lambda at: edge(p, at))
                if p.name in NORMED:
                    finish("head")
                    dve.wait_ge(taken["act"], p.nth)
                    mean_squares(BW // head_dim(p), head_dim(p), hms)
                if p.taker != "dve":
                    return
                dve.wait_ge(slab_used, p.end)
                if p.name == "ff_up":
                    b = min(p.banks)
                    dve.wait_ge(taken["act"], acts_before(p))
                    for t in range(NT):
                        ins = dve.tensor_tensor(sq[:, t, 0:p.width],
                                                pa[:, (b + t) * BW:(b + t) * BW + p.width],
                                                tok[:, t, 0:p.width], ALU.mult)
                        if t == NT - 1:
                            ins.then_inc(taken["dve"], 1)
                            dve.wait_ge(taken["dve"], p.nth)
                        else:
                            link(ins)
                    dve.sem_inc(ff_h, 1)
                elif p.name == "router":
                    at = min(p.banks) * BW
                    dve.tensor_copy(logitT, pa[0:E, at:at + SEQ]).then_inc(taken["dve"], 1)
                    visit()
                    link(dve.tensor_copy(logit, ps[:, 0:NT * E].rearrange("p (t e) -> p t e", t=NT)))
                    dve.sem_inc(side_free, 1)

            heads = 0

            def mean_squares(n, dh, ms):
                nonlocal heads
                heads += 1
                for t in range(NT):
                    ins = dve.tensor_reduce(ms[:, t * n:(t + 1) * n],
                                            sq[:, t, :].rearrange("p (h d) -> p h d", h=n),
                                            AX.X, ALU.add)
                    link(ins)
                dve.tensor_scalar(ms[:, 0:NT * n], ms[:, 0:NT * n], 1.0 / dh, EPS, ALU.mult,
                                  ALU.add).then_inc(head_ms, 1)

            def head_work(p):
                dh = head_dim(p)
                n = BW // dh
                dve.wait_ge(head_rs, heads)
                for t in range(NT):
                    v = tok[:, t, :].rearrange("p (h d) -> p h d", h=n)
                    ins = dve.tensor_tensor(v, v, hrs[:, t * n:(t + 1) * n].unsqueeze(2)
                                            .broadcast_to([P, n, dh]), ALU.mult)
                    ins.then_inc(head_scaled, 1)
                yield
                yield
                visit()
                dve.wait_ge(gains_loaded, GAINS)
                dst, g, c = {"sb_q": (qT, 0, SB_DH ** -0.5), "sb_k": (kT, 1, 1.0),
                             "ca_q": (cqT, 3, 1.0), "mem_k": (ckT, 4, 1.0)}[p.name]
                for t in range(NT):
                    ins = dve.tensor_scalar(
                        dst[:, :, t * P:(t + 1) * P],
                        ps[:, DM + t * BW:DM + (t + 1) * BW].rearrange("p (a t) -> p a t", a=4),
                        head_gains[:, p.layer, g:g + 1], c, ALU.mult, ALU.mult)
                    if t == NT - 1:
                        ins.then_inc(head_done, 1)
                        dve.wait_ge(head_done, head_number(p))
                    else:
                        link(ins)
                dve.sem_inc(side_free, 1)
                yield

            def sb_work(l):
                for c in range(SB_HEADS // 2):
                    k = 4 * l + c
                    visit()
                    z = ps[:, 0:2 * BW].rearrange("p (h n) -> p h n", h=2)[:, :, 0:384]
                    dve.wait_ge(sb_sp, k + 1)
                    dve.scalar_tensor_tensor(out=sb_u, in0=z, scalar=0.0, in1=sb_e, op0=ALU.max,
                                             op1=ALU.add).then_inc(sb_uu, 1)
                    dve.wait_ge(sb_uu, k + 1)
                    dve.sem_inc(side_free, 1)
                    yield
                    yield
                    visit()
                    dve.tensor_scalar(sb_w, z, 0.0, None, ALU.min).then_inc(sb_min, 1)
                    dve.wait_ge(sb_min, k + 1)
                    dve.sem_inc(side_free, 1)
                    yield
                    yield
                    visit()
                    dve.wait_ge(sb_hi, k + 1)
                    link(dve.tensor_tensor(ot[0][:, 1, c, :], ps[:, 0:SEQ],
                                           ot[0][:, 0, c, :].bitcast(F32), ALU.subtract))
                    dve.sem_inc(side_free, 1)
                    yield
                dve.sem_inc(branch_lo, 1)

            def gla_work(l):
                visit()
                dve.wait_ge(gla_lg, l + 1)
                dve.scalar_tensor_tensor(out=la.rearrange("p a b -> p (a b)"), in0=ps[:, 0:BW],
                                         scalar=0.0, in1=lg.rearrange("p a b -> p (a b)"),
                                         op0=ALU.min, op1=ALU.subtract).then_inc(gla_la, 1)
                dve.wait_ge(gla_la, l + 1)
                dve.sem_inc(side_free, 1)
                yield
                yield
                visit()
                dve.wait_ge(gla_exp, l + 1)
                dve.sem_inc(side_free, 1)
                link(dve.tensor_tensor(kend, gqk[:, :, 256:512], erev, ALU.mult))
                yield
                visit()
                for t in range(NT):
                    v = ps[:, t * BW:(t + 1) * BW].rearrange("p (a b t) -> p a b t", a=2, b=2)
                    cols = slice(t * P, (t + 1) * P)
                    link(dve.scalar_tensor_tensor(out=qdT[:, :, cols], in0=v[:, 0], in1=ecT[:, :, cols],
                                                  scalar=GLA_DK ** -0.5, op0=ALU.mult, op1=ALU.mult))
                    link(dve.tensor_tensor(kiT[:, :, cols], v[:, 1], einvT[:, :, cols], ALU.mult))
                dve.sem_inc(gla_dec, 1)
                dve.sem_inc(side_free, 1)
                yield
                yield
                visit()
                for c in range(3):
                    kv = ps[:, (c % 2) * BW + (c // 2) * 256:(c % 2) * BW + (c // 2) * 256 + 256]\
                        .rearrange("p (b d) -> p b d", b=2)
                    if c == 0:
                        link(dve.tensor_copy(state[:, 0], kv))
                        continue
                    last = (c + 1) * GLA_CHUNK - 1
                    for b in range(2):
                        link(dve.scalar_tensor_tensor(
                            out=state[:, c, b, :], in0=state[:, c - 1, b, :],
                            scalar=ecT[:, b, last:last + 1], in1=kv[:, b, :], op0=ALU.mult,
                            op1=ALU.add))
                dve.sem_inc(gla_state, 1)
                dve.wait_ge(gla_sc, l + 1)
                dve.sem_inc(side_free, 1)
                yield
                yield
                visit()
                dve.wait_ge(gla_o, l + 1)
                dve.sem_inc(side_free, 1)
                mean_squares(GLA_HEADS, GLA_DV, ms)
                k = heads
                yield
                dve.wait_ge(head_rs, k)
                for t in range(NT):
                    v = go[:, t, :].rearrange("p (h d) -> p h d", h=GLA_HEADS)
                    link(dve.tensor_tensor(v, v, rstd[:, t * 4:(t + 1) * 4].unsqueeze(2)
                                           .broadcast_to([P, GLA_HEADS, GLA_DV]), ALU.mult))
                dve.tensor_tensor(go, go, gr[:, :, :], ALU.mult).then_inc(gla_scaled, 1)
                yield
                yield
                visit()
                for t in range(NT):
                    cols = slice(t * P, (t + 1) * P)
                    dve.wait_ge(gla_hi, NT * l + t + 1)
                    link(dve.scalar_tensor_tensor(
                        out=ot[1][:, 1, :, cols],
                        in0=ps[:, t * BW:(t + 1) * BW].rearrange("p (h t) -> p h t", h=4),
                        scalar=head_gains[:, l, 2:3], in1=ot[1][:, 0, :, cols].bitcast(F32),
                        op0=ALU.mult, op1=ALU.subtract))
                dve.sem_inc(side_free, 1)
                dve.sem_inc(branch_lo, 1)
                yield

            def ca_work(l):
                n = NT * CA_HEADS
                yield from pause(CA_DELAY)
                visit()
                link(dve.tensor_reduce(ms[:, 0:n], ps[:, :].rearrange("p (a m) -> p a m", a=n), AX.X,
                                       ALU.max))
                dve.tensor_scalar(ms[:, 0:n], ms[:, 0:n], -CA_DH ** -0.5, None, ALU.mult)\
                    .then_inc(ca_max, 1)
                yield
                yield
                dve.wait_ge(ca_exp, l + 1)
                dve.sem_inc(side_free, 1)
                link(dve.reciprocal(rstd[:, 0:n], rstd[:, 0:n]))
                yield
                dve.tensor_tensor(probs, probs, rstd[:, 0:n].unsqueeze(2).broadcast_to([P, n, MEM]),
                                  ALU.mult).then_inc(ca_scaled, 1)
                yield
                visit()
                dve.tensor_copy(pT[:, 1, :, :].rearrange("p h t -> p (h t)"), ps[:, 2 * BW:4 * BW])\
                    .then_inc(ca_ptv, 1)
                dve.wait_ge(ca_pt, l + 1)
                dve.wait_ge(ca_ptv, l + 1)
                dve.sem_inc(side_free, 1)
                yield
                yield
                visit()
                dve.wait_ge(ca_hi, l + 1)
                link(dve.tensor_tensor(ot[0][:, 1, :, :].rearrange("p h t -> p (h t)"),
                                       ps[:, 0:2 * BW],
                                       ot[0][:, 0, :, :].rearrange("p h t -> p (h t)").bitcast(F32),
                                       ALU.subtract))
                dve.sem_inc(side_free, 1)
                dve.sem_inc(branch_lo, 1)
                yield

            blocks = 0

            def ff_work(width, k0):
                nonlocal blocks
                blocks += 1
                visit()
                n = width // P
                for t in range(NT):
                    cols = slice(t * P, (t + 1) * P)
                    dve.wait_ge(ff_hi, NT * (blocks - 1) + t + 1)
                    ins = dve.tensor_tensor(
                        ht[:, 1, k0:k0 + n, cols],
                        ps[:, t * BW:t * BW + width].rearrange("p (k t) -> p k t", k=n),
                        ht[:, 0, k0:k0 + n, cols].bitcast(F32), ALU.subtract)
                    ins.then_inc(ff_lo, 1)
                dve.wait_ge(ff_lo, NT * blocks)
                dve.sem_inc(side_free, 1)
                yield

            def side_work(p):
                l = p.layer
                for name in side_names(p):
                    yield name, (head_work(p) if name == "head" else sb_work(l) if name == "sb"
                                 else gla_work(l) if name == "gla" else ca_work(l) if name == "ca"
                                 else ff_work(p.width, hidden_tile(p)))

            in_order(side_work, product, {"start": start, "memory": memory, "x_norm": x_norm,
                                          "x_turn": x_turn, "ffn_tokens": ffn_norm})

            dve.wait_ge(r_const, 1)
            for t in range(NT):
                link(dve.max(top[:, t, :], logit[:, t, :]))
                link(dve.max_index(topu[:, t, :], top[:, t, :], logit[:, t, :]))
            link(dve.tensor_copy(topi, topu[:, :, :]))
            every = iota_e.unsqueeze(1).broadcast_to([P, NT, E])
            link(dve.tensor_tensor(pick1, every, topi[:, :, 0:1].broadcast_to([P, NT, E]),
                                   ALU.is_equal))
            link(dve.tensor_tensor(pick2, every, topi[:, :, 1:2].broadcast_to([P, NT, E]),
                                   ALU.is_equal))
            link(dve.tensor_tensor(wd.unsqueeze(2), top[:, :, 1:2], top[:, :, 0:1], ALU.subtract))
            dve.tensor_tensor(assign, pick1, pick2, ALU.add).then_inc(r_assign, 1)
            link(dve.memset(slot_pos, -1.0))
            link(dve.memset(slot_comb, 0.0))
            link(dve.memset(ozero, 0.0))
            dve.memset(selT.bitcast(F32), 0.0).then_inc(selt_ready, 1)
            visit()
            pos = slot_pos[:, :, 0:E]
            link(dve.scalar_tensor_tensor(out=pos, in0=ps[:, 0:NT * E]
                                          .rearrange("p (t e) -> p t e", t=NT), scalar=1.0,
                                          in1=assign, op0=ALU.add, op1=ALU.mult))
            link(dve.tensor_scalar(pos, pos, 1.0, None, ALU.subtract))
            for t in range(NT):
                dve.tensor_scalar(sel[:, t, :], iota_c[:, :], slot_pos[:, t, 0:1], None,
                                  ALU.is_equal).then_inc(sel_ready, 1)
            link(dve.tensor_scalar(over, ps[:, NT * E:(NT + 1) * E], float(CAP), None, ALU.is_gt))
            link(dve.tensor_tensor_scan(oidx, over, ozero, 0.0, ALU.add, ALU.add))
            link(dve.tensor_scalar(slotf[:, 0:1], oidx[:, E - 1:E], float(E), None, ALU.add))
            three = [P, OVER, E]
            link(dve.tensor_tensor(mk, oidx.unsqueeze(1).broadcast_to(three),
                                   order.unsqueeze(2).broadcast_to(three), ALU.is_equal))
            link(dve.tensor_tensor(mk, mk, over.unsqueeze(1).broadcast_to(three), ALU.mult))
            link(dve.tensor_tensor(mtmp, mk, iota_e.unsqueeze(1).broadcast_to(three), ALU.mult))
            link(dve.tensor_reduce(slotf[:, 1:1 + OVER], mtmp, AX.X, ALU.add))
            dve.tensor_copy(slot_i[0:1, :], slotf[0:1, :]).then_inc(r_table, 1)
            for t in range(NT):
                dve.wait_ge(r_hi, t + 1)
                dve.tensor_tensor(th[:, 1, t, :], hn[:, t, :], th[:, 0, t, :].bitcast(F32),
                                  ALU.subtract).then_inc(r_lo, 1)
            dve.wait_ge(r_wd, 1)
            link(dve.tensor_scalar(w1, wd, 1.0, None, ALU.add))
            link(dve.reciprocal(w1, w1))
            link(dve.tensor_tensor(w2, w1, wd, ALU.mult))
            link(dve.tensor_tensor(pick1, pick1, w1.unsqueeze(2).broadcast_to([P, NT, E]), ALU.mult))
            link(dve.tensor_tensor(pick2, pick2, w2.unsqueeze(2).broadcast_to([P, NT, E]), ALU.mult))
            comb = slot_comb[:, :, 1:1 + E]
            link(dve.tensor_tensor(comb, pick1, pick2, ALU.add))
            for t in range(NT):
                link(dve.tensor_tensor(mtmp, mk, pos[:, t:t + 1, :].broadcast_to(three), ALU.mult))
                link(dve.tensor_reduce(slot_pos[:, t, E:SLOTS], mtmp, AX.X, ALU.add))
                link(dve.tensor_scalar(slot_pos[:, t, E:SLOTS], slot_pos[:, t, E:SLOTS], float(CAP),
                                       None, ALU.subtract))
                link(dve.tensor_tensor(mtmp, mk, comb[:, t:t + 1, :].broadcast_to(three), ALU.mult))
                link(dve.tensor_reduce(slot_comb[:, t, 1 + E:1 + SLOTS], mtmp, AX.X, ALU.add))
            dve.memset(ps[:, 0:DM], 0.0).then_inc(y_cleared, 1)
            dve.wait_ge(gathered, 2)
            dve.tensor_copy(xg[:, 1, :, :].rearrange("p k c -> p (k c)"), pa[:, DM:2 * DM])\
                .then_inc(xg_lo, 1)

            dve.wait_ge(r_table, 1)
            slots = dve.value_load(slot_i[0:1, 0:1], min_val=EXPERTS, max_val=SLOTS)

            def output_lo(n):
                dve.wait_ge(y_hi, n)
                dve.tensor_tensor(ysp[:, 1, :], ps[:, 0:DM], ysp[:, 0, :].bitcast(F32),
                                  ALU.subtract).then_inc(y_lo, 1)

            def add_slot(i):
                for t in range(NT):
                    dve.wait_ge(scattered, i * NT + (t + 1))
                    q = (1 - t) * DM
                    dve.scalar_tensor_tensor(out=xs[:, t, :], in0=ps[:, q:q + DM],
                                             scalar=slot_comb[:, t, bass.ds(i, 1)],
                                             in1=xs[:, t, :], op0=ALU.mult, op1=ALU.add)\
                        .then_inc(added, 1)

            with dve.Fori(0, slots) as i:
                at = i * EXP_SLABS
                j = 0

                def expert_split(n):
                    nonlocal j
                    while j < min(n, EXP_SLABS):
                        s = PRE + j
                        dve.wait_ge(hi_ready, at + (s + 1))
                        dve.tensor_tensor(exp_lo[j % EXP_SPLIT], exp_slots[j % EXP_RAW][0],
                                          exp_hi[j % EXP_SPLIT].bitcast(F32), ALU.subtract)\
                            .then_inc(lo_ready, 1)
                        j += 1

                expert_split(EXP_AHEAD)
                output_lo(i + 1)
                used = 0
                for s in range(STEPS + 1):
                    if s < STEPS:
                        for _ in range(GU):
                            used += 1
                            expert_split(used + EXP_AHEAD)
                    if s > 0:
                        dve.wait_ge(e_hi, i * STEPS + s)
                        v = hts[buf[s - 1]][:, :, :, :].rearrange("p s k c -> p s (k c)")
                        dve.tensor_tensor(v[:, 1, :], pa[:, 3 * BW:4 * BW],
                                          v[:, 0, :].bitcast(F32), ALU.subtract).then_inc(e_lo, 1)
                    else:
                        add_slot(i)
                    if s < STEPS:
                        for _ in range(GU):
                            used += 1
                            expert_split(used + EXP_AHEAD)
                        dve.wait_ge(slab_used, at + (PRE + used))
                        dve.wait_ge(e_silu, i * STEPS + (s + 1))
                        if s > 0:
                            dve.wait_ge(e_turned, i * STEPS + s)
                        dve.tensor_tensor(hb, pa[:, BW:2 * BW], hs, ALU.mult).then_inc(e_h, 1)
                    if s == 1:
                        dve.wait_ge(selt_turned, i + 1)
                        for t in range(NT):
                            dve.tensor_scalar(sel[:, t, :], iota_c[:, :],
                                              slot_pos[:, t, bass.ds(i + 1, 1)], None,
                                              ALU.is_equal).then_inc(sel_ready, 1)
                    if s > 0:
                        for _ in range(HT):
                            used += 1
                            expert_split(used + EXP_AHEAD)
                dve.wait_ge(gathered, i * 2 + 4)
                dve.tensor_copy(xg[:, 1, :, :].rearrange("p k c -> p (k c)"), ps[:, DM:2 * DM])\
                    .then_inc(xg_lo, 1)
            for c in range(2):
                cols = slice(c * BW, (c + 1) * BW)
                dve.wait_ge(y_hi, slots + (c + 1))
                dve.tensor_tensor(ysp[:, 1, cols], ps[:, cols], ysp[:, 0, cols].bitcast(F32),
                                  ALU.subtract).then_inc(y_lo, 1)
            add_slot(slots)

        @block.tensor
        def _(pe):
            frees = 0

            def enter():
                nonlocal frees
                if frees:
                    pe.wait_ge(side_free, frees)
                frees += 1

            lhs_of = {"xt0": xt0, "xt1": xt1, "ot0": ot[0], "ot1": ot[1], "ht": ht}

            norms = turns = ffs = 0

            def turn_tokens(normed, banks, t):
                nonlocal norms, turns
                if banks is ps and t == 0:
                    enter()
                if normed:
                    norms += 1
                    pe.wait_ge(norm_done, norms)
                for k in range(KT):
                    ins = pe.transpose(banks[:, t * DM + k * P:t * DM + (k + 1) * P],
                                       hn[:, t, k * P:(k + 1) * P], ident[:, :])
                ins.then_inc(turn_ready, 1)
                turns += 1

            def start():
                pe.wait_ge(consts, 1)
                for t in range(NT):
                    turn_tokens(True, ps, t)

            def memory(l):
                yield
                for t in range(NT):
                    turn_tokens(True, ps, t)
                yield

            def x_norm(l):
                pass

            def x_turn(l):
                yield
                for t in range(NT):
                    turn_tokens(True, ps, t)
                yield

            def ffn_norm(l):
                turn_tokens(True, ps, 0)
                if l == LAYERS - 1:
                    turn_tokens(True, ps, 1)

            def merged_turn(l, t):
                pe.wait_ge(merge_step, NT * (BRANCHES * (l + 1) - 1) + t + 1)
                turn_tokens(False, ps, t)

            def passes(dst, hi, lo, m_hi, m_lo, first, last):
                pe.matmul(dst, hi, m_hi, start=first, stop=False)
                pe.matmul(dst, hi, m_lo, start=False, stop=False)
                return pe.matmul(dst, lo, m_hi, start=False, stop=last)

            def product(p, side, finish):
                if p.name.startswith("branch"):
                    pe.wait_ge(branch_lo, BRANCHES * p.layer + int(p.name[-1]) + 1)
                lhs = lhs_of[p.lhs]
                b = min(p.banks)
                kts = len(p.slabs) * max(1, SLAB // p.width) if p.width >= 256 else KT
                per = kts // len(p.slabs)

                def ready(tiles):
                    if p.kind == "cols":
                        banks = {b + t for t in tiles}
                    else:
                        banks = {b + 2 * t + c for t in tiles for c in range(2)}
                    for q in p.before:
                        both = q.banks & banks
                        if both and q.kind == "cols":
                            pe.wait_ge(taken[q.taker], q.nth)
                        elif both:
                            t = (max(both) - min(q.banks)) // 2
                            pe.wait_ge(taken["rows"], NT * (q.nth - 1) + t + 1)
                    if p.lhs in ("xt0", "xt1"):
                        pe.wait_ge(turn_lo, turns)

                def multiply(n, tiles):
                    s = p.first + n
                    pe.wait_ge(lo_ready, s + 1)
                    if p.width < P:
                        for k in range(KT):
                            at = slice(k * p.width, (k + 1) * p.width)
                            ins = passes(pa[0:p.width, b * BW:b * BW + SEQ], w_hi[:, s % SPLIT, at],
                                         w_lo[:, s % SPLIT, at], lhs[:, 0, k, :], lhs[:, 1, k, :],
                                         k == 0, k == KT - 1)
                        return ins
                    if p.name == "ff_down":
                        pe.wait_ge(ff_lo, NT * (hidden_before(p) + n // HT + 1))
                    for kk in range(per):
                        k = n * per + kk
                        for t in tiles:
                            hi, lo = (lhs[:, h, k, t * P:(t + 1) * P] for h in range(2))
                            for c in range(0, p.width, BW):
                                w = min(BW, p.width - c)
                                at = kk * p.width + c
                                if p.kind == "cols":
                                    dst = pa[:, (b + t) * BW:(b + t) * BW + w]
                                else:
                                    dst = pa[:, t * DM + c:t * DM + c + w]
                                ins = passes(dst, hi, lo, w_hi[:, s % SPLIT, at:at + w],
                                             w_lo[:, s % SPLIT, at:at + w], k == 0, k == kts - 1)
                    return ins

                for g, group in enumerate(p.groups):
                    if g not in p.by_tile:
                        if g == 0:
                            ready(range(NT))
                        multiply(group[0], range(NT)).then_inc(slab_used, 1)
                        side()
                        continue
                    for t in range(NT):
                        if g == 0:
                            ready([t])
                        for i, n in enumerate(group):
                            ins = multiply(n, [t])
                            last = n == group[-1]
                            if t == NT - 1:
                                ins.then_inc(slab_used, 1)
                            elif last and p.kind == "rows" and g == len(p.groups) - 1:
                                ins.then_inc(tile_done, 1)
                            if i in ((1, 3), (1, 2))[t]:
                                side()
                            if t == 0 and g == 0 and i == 1:
                                if p.name == "out":
                                    merged_turn(p.layer, 1)
                                elif p is first_gate:
                                    turn_tokens(True, ps, 1)
                            if (p.name, t, i) == ("branch2", 1, 2):
                                merged_turn(p.layer, 0)
                if p.name in NORMED:
                    finish("head")

            headed = 0

            def head_work():
                nonlocal headed
                yield
                yield
                enter()
                for t in range(NT):
                    headed += 1
                    pe.wait_ge(head_scaled, headed)
                    for a in range(4):
                        ins = pe.transpose(ps[:, DM + t * BW + a * P:DM + t * BW + (a + 1) * P],
                                           tok[:, t, a * P:(a + 1) * P], ident[:, :])
                ins.then_inc(side_ready, 1)
                yield

            def mm(dst, a, b, start, stop):
                return pe.matmul(dst, a, b, start=start, stop=stop, skip_group_check=True)

            def sb_work(l):
                for c in range(SB_HEADS // 2):
                    k = 4 * l + c
                    if c == 0:
                        pe.wait_ge(consts, 2)
                        pe.wait_ge(gains_loaded, GAINS)
                        pe.wait_ge(head_done, len(NORMED) * l + 3)
                        pe.wait_ge(taken["act"], nth_of("sb_v", l))

                    enter()
                    for h in range(2):
                        r = slice(h * SB_DH, (h + 1) * SB_DH)
                        mm(ps[:, h * BW:h * BW + SEQ], kT[r, c, 0:P], qT[r, c, :], True, True)
                        ins = mm(ps[:, h * BW + SEQ:h * BW + 384], kT[r, c, P:SEQ],
                                 qT[r, c, P:SEQ], False, True)
                    ins.then_inc(side_ready, 1)
                    yield
                    yield
                    enter()
                    pe.wait_ge(sb_um, k + 1)
                    for h in range(2):
                        mm(ps[:, h * BW:h * BW + 384], neg_tri[:, :], sb_u[:, h, :], False, False)
                        ins = mm(ps[:, h * BW + P:h * BW + SEQ], neg_one[:, :], sb_u[:, h, SEQ:384],
                                 False, True)
                    ins.then_inc(side_ready, 1)
                    yield
                    yield
                    enter()
                    pe.wait_ge(sb_wm, k + 1)
                    for h in range(2):
                        r = slice(h * SB_DH, (h + 1) * SB_DH)
                        v = slice((2 * c + h) * SB_DH, (2 * c + h + 1) * SB_DH)
                        mm(ps[r, 0:SEQ], sv[:, 0, v], sb_w[:, h, 0:SEQ], True, False)
                        ins = mm(ps[r, P:SEQ], sv[:, 1, v], sb_w[:, h, SEQ:384], False, True)
                    ins.then_inc(side_ready, 1)
                    yield

            def gla_work(l):
                enter()
                pe.wait_ge(taken["act"], nth_of("gla_r", l))
                for t in range(NT):
                    dst = ps[:, t * 256:(t + 1) * 256]
                    ins = mm(dst, gaT[:, t * P:(t + 1) * P], a_up[:, l, :], t == 0, True)
                ins.then_inc(side_ready, 1)
                yield
                yield
                enter()
                pe.wait_ge(gla_la, l + 1)
                for b in range(2):
                    for t in range(NT):
                        mm(ps[:, b * SEQ + t * P:b * SEQ + (t + 1) * P], la[:, t, b * P:(b + 1) * P],
                           cum_tri[:, :], b == 0 and t == 0, True)
                for t in range(NT):
                    ins = mm(ps[:, BW + t * 256:BW + (t + 1) * 256], rev_tri[:, :], la[:, t, :],
                             t == 0, True)
                ins.then_inc(side_ready, 1)
                yield
                enter()
                for t in range(NT):
                    for a in range(4):
                        ins = pe.transpose(ps[:, t * BW + a * P:t * BW + (a + 1) * P],
                                           gqk[:, t, a * P:(a + 1) * P], ident[:, :])
                ins.then_inc(side_ready, 1)
                yield
                yield
                enter()
                pe.wait_ge(gla_dec, l + 1)
                for b in range(2):
                    for t in range(NT):
                        for h in range(2):
                            r = slice(h * GLA_DK, (h + 1) * GLA_DK)
                            cols = slice(t * P, (t + 1) * P)
                            at = (2 + h) * BW + (b * NT + t) * P
                            mm(ps[:, at:at + P], kiT[r, b, cols], qdT[r, b, cols],
                               b == 0 and t == 0, True)
                for c in range(3):
                    t, r = c // 2, slice((c % 2) * GLA_CHUNK, (c % 2 + 1) * GLA_CHUNK)
                    for b in range(2):
                        for h in range(2):
                            head = 2 * b + h
                            at = (c % 2) * BW + (c // 2) * 256 + b * GLA_DV
                            ins = mm(ps[h * GLA_DK:(h + 1) * GLA_DK, at:at + GLA_DV],
                                     kend[r, t, head * GLA_DK:(head + 1) * GLA_DK],
                                     gv[r, t, head * GLA_DV:(head + 1) * GLA_DV],
                                     c < 2 and b == 0, True)
                ins.then_inc(side_ready, 1)
                yield
                yield
                enter()
                pe.wait_ge(gla_mask, l + 1)
                pe.wait_ge(gla_state, l + 1)
                for b in range(2):
                    for t in range(NT):
                        for h in range(2):
                            head, at = 2 * b + h, h * BW + (b * NT + t) * P
                            mm(ps[:, at:at + P], scT[:, h * 4 + b * NT + t, :],
                               gv[:, t, head * GLA_DV:(head + 1) * GLA_DV], b == 0 and t == 0, False)
                for b in range(2):
                    for c in range(1, 4):
                        for h in range(2):
                            r = slice(h * GLA_DK, (h + 1) * GLA_DK)
                            o = slice((c % 2) * GLA_CHUNK, (c % 2 + 1) * GLA_CHUNK)
                            at = h * BW + (b * NT + c // 2) * P
                            ins = mm(ps[o, at:at + P], qdT[r, b, c * GLA_CHUNK:(c + 1) * GLA_CHUNK],
                                     state[r, c - 1, b, :], False, True)
                ins.then_inc(side_ready, 1)
                yield
                yield
                yield
                enter()
                pe.wait_ge(gla_scaled, l + 1)
                for t in range(NT):
                    for a in range(4):
                        ins = pe.transpose(ps[:, t * BW + a * P:t * BW + (a + 1) * P],
                                           go[:, t, a * P:(a + 1) * P], ident[:, :])
                ins.then_inc(side_ready, 1)
                yield

            def ca_work(l):
                yield from pause(CA_DELAY)
                enter()
                pe.wait_ge(head_done, len(NORMED) * (l + 1))
                for t in range(NT):
                    for h in range(CA_HEADS):
                        at = (t * CA_HEADS + h) * MEM
                        ins = mm(ps[:, at:at + MEM], cqT[:, h, t * P:(t + 1) * P], ckT[:, h, :],
                                 h % 2 == 0, True)
                ins.then_inc(side_ready, 1)
                yield
                yield
                yield
                yield
                enter()
                pe.wait_ge(ca_scaled, l + 1)
                for m in range(NT):
                    for t in range(NT):
                        for h in range(CA_HEADS):
                            at = m * 2 * BW + h * SEQ + t * P
                            ins = pe.transpose(ps[:, at:at + P],
                                               probs[:, t * CA_HEADS + h, m * P:(m + 1) * P],
                                               ident[:, :])
                ins.then_inc(side_ready, 1)
                yield
                yield
                enter()
                pe.wait_ge(ca_pt, l + 1)
                pe.wait_ge(ca_ptv, l + 1)
                for h in range(CA_HEADS):
                    for m in range(NT):
                        ins = mm(ps[:, h * SEQ:(h + 1) * SEQ], cv[:, m, h * CA_DH:(h + 1) * CA_DH],
                                 pT[:, m, h, :], h % 2 == 0 and m == 0, m == NT - 1)
                ins.then_inc(side_ready, 1)
                yield

            def ff_work(width):
                nonlocal ffs
                ffs += 1
                enter()
                pe.wait_ge(ff_h, ffs)
                for t in range(NT):
                    for a in range(width // P):
                        ins = pe.transpose(ps[:, t * BW + a * P:t * BW + (a + 1) * P],
                                           sq[:, t, a * P:(a + 1) * P], ident[:, :])
                ins.then_inc(side_ready, 1)
                yield

            def side_work(p):
                l = p.layer
                for name in side_names(p):
                    yield name, (head_work() if name == "head" else sb_work(l) if name == "sb"
                                 else gla_work(l) if name == "gla" else ca_work(l) if name == "ca"
                                 else ff_work(p.width))

            in_order(side_work, product, {"start": start, "memory": memory, "x_norm": x_norm,
                                          "x_turn": x_turn, "ffn_tokens": ffn_norm})

            enter()
            pe.wait_ge(taken["dve"], table[-1].nth)
            for t in range(NT):
                ins = pe.transpose(ps[:, t * E:(t + 1) * E], logitT[:, t * P:(t + 1) * P],
                                   ident[0:E, 0:E])
            ins.then_inc(side_ready, 1)
            enter()
            pe.wait_ge(r_assign, 1)
            mm(ps[:, 0:E], utri[:, :], assign[:, 0, :], True, True)
            mm(ps[:, E:2 * E], ones[:, :], assign[:, 0, :], False, False)
            mm(ps[:, E:2 * E], utri[:, :], assign[:, 1, :], False, True)
            mm(ps[:, 2 * E:3 * E], ones[:, :], assign[:, 0, :], False, False)
            mm(ps[:, 2 * E:3 * E], ones[:, :], assign[:, 1, :], False, True).then_inc(side_ready, 1)

            def gather(n, h, banks=ps):
                pe.wait_ge(sel_ready, n * NT + NT)
                for k in range(KT):
                    for t in range(NT):
                        ins = mm(banks[:, DM + k * P:DM + (k + 1) * P],
                                 th[:, h, t, k * P:(k + 1) * P], sel[:, t, :],
                                 k % 4 == 0 and t == 0, t == NT - 1)
                ins.then_inc(gathered, 1)

            def scatter(n, halves=1):
                pe.wait_ge(selt_ready, n + 1)
                pe.wait_ge(y_lo, n + halves)
                for t in range(NT):
                    for c in range(2):
                        for h in range(2):
                            dst = (1 - t) * DM + c * BW
                            ins = mm(ps[:, dst:dst + BW], selT[:, t * P:(t + 1) * P],
                                     ysp[:, h, c * BW:(c + 1) * BW], h == 0, h == 1)
                    ins.then_inc(scattered, 1)

            pe.wait_ge(r_hi, NT)
            gather(0, 0)
            pe.wait_ge(r_lo, NT)
            gather(0, 1, pa)
            pe.wait_ge(r_table, 1)
            slots = pe.value_load(slot_i[0:1, 0:1], min_val=EXPERTS, max_val=SLOTS)
            with pe.Fori(0, slots) as i:
                at = i * EXP_SLABS
                j = 0

                def block_of(bank):
                    nonlocal j
                    n = SLAB // BW
                    for q in range(GU):
                        s = PRE + j
                        pe.wait_ge(lo_ready, at + (s + 1))
                        for kk in range(n):
                            k = q * n + kk
                            cols = slice(kk * BW, (kk + 1) * BW)
                            ins = passes(pa[:, bank * BW:(bank + 1) * BW], xg[:, 0, k, :],
                                         xg[:, 1, k, :], exp_hi[j % EXP_SPLIT][:, cols],
                                         exp_lo[j % EXP_SPLIT][:, cols], k == 0, k == KT - 1)
                        ins.then_inc(slab_used, 1)
                        j += 1

                def down(s):
                    nonlocal j
                    pe.wait_ge(e_lo, i * STEPS + (s + 1))
                    for k in range(HT):
                        q = PRE + j
                        pe.wait_ge(lo_ready, at + (q + 1))
                        for c in range(0, DM, BW):
                            ins = passes(ps[:, c:c + BW], hts[buf[s]][:, 0, k, :],
                                         hts[buf[s]][:, 1, k, :],
                                         exp_hi[j % EXP_SPLIT][:, c:c + BW],
                                         exp_lo[j % EXP_SPLIT][:, c:c + BW], s == 0 and k == 0,
                                         s == STEPS - 1 and k == HT - 1)
                        ins.then_inc(slab_used, 1)
                        j += 1

                for s in range(STEPS + 1):
                    if s == 0:
                        pe.wait_ge(xg_hi, i + 1)
                        pe.wait_ge(xg_lo, i + 1)
                    if s < STEPS:
                        if s > 0:
                            pe.wait_ge(e_silu, i * STEPS + s)
                        block_of(0)
                    if s == 0:
                        scatter(i)
                        for t in range(NT):
                            ins = pe.transpose(pa[:, 2 * BW + t * P:2 * BW + (t + 1) * P],
                                               sel[:, t, :].bitcast(F32), ident[:, :])
                        ins.then_inc(selt_turned, 1)
                    else:
                        pe.wait_ge(e_h, i * STEPS + s)
                        if s > 1:
                            pe.wait_ge(e_lo, i * STEPS + (s - 1))
                        for a in range(HT):
                            ins = pe.transpose(pa[:, 3 * BW + a * P:3 * BW + (a + 1) * P],
                                               hb[:, a * P:(a + 1) * P], ident[:, :])
                        ins.then_inc(e_turned, 1)
                    if s < STEPS:
                        block_of(1)
                    if s == 1:
                        pe.wait_ge(added, i * NT + NT)
                    if s == 2:
                        gather(i + 1, 0)
                    if s == STEPS:
                        pe.wait_ge(xg_hi, i + 2)
                        gather(i + 1, 1)
                    if s > 0:
                        down(s - 1)
            scatter(slots, 2)


_INS = ["x", "mem", "mix_norm_g", "w_in", "sb_q_g", "sb_k_g", "gla_a_up", "gla_a_b", "gla_o_g",
        "ca_q_g", "ca_k_g", "mem_norm_g", "w_mem_kv", "w_br_sb", "w_br_gla", "w_br_ca", "w_out",
        "ffn_norm_g", "ff_w_gate_up", "ff_w_down", "moe_w_router", "moe_w_gate_up", "moe_w_down"]


def kernel(**inputs):
    import numpy as np
    from concourse import bacc
    from concourse.bass_utils import run_bass_kernel_spmd

    nc = bacc.Bacc("TRN2", target_bir_lowering=False, num_devices=1)
    arrays, args = {}, []
    for name in _INS:
        a = np.ascontiguousarray(inputs[name])
        arrays[f"in_{name}"] = a
        args.append(nc.dram_tensor(f"in_{name}", a.shape, mybir.dt.from_np(a.dtype),
                                   kind="ExternalInput").ap())
    out = nc.dram_tensor("out", [1, SEQ, DM], F32, kind="ExternalOutput").ap()
    trunk(nc, *args, out)
    return run_bass_kernel_spmd(nc, [arrays], core_ids=[0]).results[0]["out"]
```
